# Optimizing a Trainium2 kernel written in Bass

```python
import math
import jax, jax.numpy as jnp
from jax import lax
import numpy as np

D_MODEL = 2048
BATCH = 1
SEQ = 256
DEPTH = 2

EPS = 1e-6
NEG_INF = -1e30

SSM_WIDTH = D_MODEL // 2
SSM_GROUP = 16
SSM_GROUPS = SSM_WIDTH // SSM_GROUP
SSM_STATE = 64
DT_MIN = 1e-3
DT_MAX = 1e-1

SG_WIDTH = D_MODEL // 2
SG_HEADS = 8
SG_HEAD_DIM = SG_WIDTH // SG_HEADS
SG_CHUNK = 128

HEAD_DIM = 64
ATT_HEADS = D_MODEL // 128
ATT_KV_HEADS = ATT_HEADS // 8
GQA_GROUP = ATT_HEADS // ATT_KV_HEADS
ATT_WIDTH = ATT_HEADS * HEAD_DIM
KV_WIDTH = ATT_KV_HEADS * HEAD_DIM
WINDOW = 128
ATT_BLOCK = 128
ROT_DIM = HEAD_DIM // 4
ROPE_THETA = 500000.0

N_BRANCH = 3
IN_SIZES = (SSM_WIDTH, SSM_WIDTH, SG_WIDTH, SG_WIDTH, SG_WIDTH,
            ATT_WIDTH, KV_WIDTH, KV_WIDTH, ATT_WIDTH, N_BRANCH * D_MODEL)
D_IN = sum(IN_SIZES)
IN_OFFSETS = tuple(sum(IN_SIZES[:i + 1]) for i in range(len(IN_SIZES) - 1))

kernel_name = "hybrid_s5_gmlp_swa_gated_block"

def rmsnorm(x, w):
    xf = x.astype(jnp.float32)
    y = xf * lax.rsqrt(jnp.mean(xf * xf, axis=-1, keepdims=True) + EPS)
    return (y * w.astype(jnp.float32)).astype(x.dtype)

def layernorm(x, w, b):
    xf = x.astype(jnp.float32)
    mu = jnp.mean(xf, axis=-1, keepdims=True)
    var = jnp.mean(jnp.square(xf - mu), axis=-1, keepdims=True)
    y = (xf - mu) * lax.rsqrt(var + EPS)
    return (y * w.astype(jnp.float32) + b.astype(jnp.float32)).astype(x.dtype)

def partial_rope(t, pos):
    tf = t.astype(jnp.float32)
    half = ROT_DIM // 2
    inv_freq = ROPE_THETA ** (-jnp.arange(0, ROT_DIM, 2, dtype=jnp.float32) / ROT_DIM)
    ang = pos.astype(jnp.float32)[:, None] * inv_freq[None, :]
    cos = jnp.cos(ang)[None, :, None, :]
    sin = jnp.sin(ang)[None, :, None, :]
    t1 = tf[..., :half]
    t2 = tf[..., half:ROT_DIM]
    rot = jnp.concatenate([t1 * cos - t2 * sin, t2 * cos + t1 * sin, tf[..., ROT_DIM:]], axis=-1)
    return rot.astype(t.dtype)

def s5_mixer(u, a_re, a_im, log_dt, b_re, b_im, c_re, c_im, d, glu_w, glu_b):
    bsz, L, _ = u.shape
    uf = u.astype(jnp.float32).reshape(bsz, L, SSM_GROUPS, SSM_GROUP)
    lam = lax.complex(a_re.astype(jnp.float32), a_im.astype(jnp.float32))
    dt = jnp.exp(log_dt.astype(jnp.float32))[:, None]
    lam_bar = jnp.exp(lam * dt)
    b = lax.complex(b_re.astype(jnp.float32), b_im.astype(jnp.float32))
    b_bar = ((lam_bar - 1.0) / lam)[..., None] * b
    bu = jnp.einsum('blgc,gpc->blgp', uf.astype(jnp.complex64), b_bar)
    a = jnp.broadcast_to(lam_bar, bu.shape)

    def combine(e1, e2):
        a1, b1 = e1
        a2, b2 = e2
        return a1 * a2, a2 * b1 + b2

    _, states = lax.associative_scan(combine, (a, bu), axis=1)
    c = lax.complex(c_re.astype(jnp.float32), c_im.astype(jnp.float32))
    y = jnp.real(jnp.einsum('blgp,gcp->blgc', states, c))
    y = y + d.astype(jnp.float32).reshape(SSM_GROUPS, SSM_GROUP) * uf
    y = jax.nn.gelu(y.reshape(bsz, L, SSM_WIDTH)).astype(u.dtype)
    return y * jax.nn.sigmoid(y @ glu_w + glu_b)

def spatial_gating(u, v, ln_w, ln_b, w_s, b_s):
    bsz, L, _ = u.shape
    n = L // SG_CHUNK
    v = layernorm(v, ln_w, ln_b)
    vc = v.reshape(bsz, n, SG_CHUNK, SG_HEADS, SG_HEAD_DIM)
    causal = jnp.tril(jnp.ones((SG_CHUNK, SG_CHUNK), dtype=bool))
    w = jnp.where(causal[None], w_s, jnp.zeros_like(w_s))
    mixed = jnp.einsum('hts,bnshc->bnthc', w, vc) + b_s.T[:, :, None]
    return u * mixed.reshape(bsz, L, SG_WIDTH)

def sliding_window_attention(q, k, v, sinks):
    bsz, L, _ = q.shape
    n = L // ATT_BLOCK
    pos = jnp.arange(L)
    q = partial_rope(q.reshape(bsz, L, ATT_HEADS, HEAD_DIM), pos)
    k = partial_rope(k.reshape(bsz, L, ATT_KV_HEADS, HEAD_DIM), pos)
    v = v.reshape(bsz, L, ATT_KV_HEADS, HEAD_DIM)

    def banded(t):
        tp = jnp.pad(t, ((0, 0), (ATT_BLOCK, 0), (0, 0), (0, 0)))
        prev = tp[:, :L].reshape(bsz, n, ATT_BLOCK, ATT_KV_HEADS, HEAD_DIM)
        cur = t.reshape(bsz, n, ATT_BLOCK, ATT_KV_HEADS, HEAD_DIM)
        return jnp.concatenate([prev, cur], axis=2)

    kb = banded(k)
    vb = banded(v)
    qb = q.reshape(bsz, n, ATT_BLOCK, ATT_KV_HEADS, GQA_GROUP, HEAD_DIM)
    s = jnp.einsum('bnqkgd,bnskd->bnkgqs', qb, kb).astype(jnp.float32) * (HEAD_DIM ** -0.5)
    blk = jnp.arange(n)[:, None, None]
    qpos = blk * ATT_BLOCK + jnp.arange(ATT_BLOCK)[None, :, None]
    kpos = (blk - 1) * ATT_BLOCK + jnp.arange(2 * ATT_BLOCK)[None, None, :]
    diff = qpos - kpos
    allowed = (diff >= 0) & (diff < WINDOW) & (kpos >= 0)
    s = jnp.where(allowed[None, :, None, None], s, NEG_INF)
    sink = sinks.astype(jnp.float32).reshape(ATT_KV_HEADS, GQA_GROUP)[None, None, :, :, None, None]
    sink = jnp.broadcast_to(sink, s.shape[:-1] + (1,))
    p = jax.nn.softmax(jnp.concatenate([s, sink], axis=-1), axis=-1)[..., :-1]
    o = jnp.einsum('bnkgqs,bnskd->bnqkgd', p.astype(vb.dtype), vb)
    return o.reshape(bsz, L, ATT_WIDTH)

def setup_inputs(seed: int = 0) -> dict:
    key = jax.random.key(seed)
    ks = jax.random.split(key, 24)
    f32 = jnp.float32
    nrm = lambda k, shape, scale: jax.random.normal(k, shape, f32) * scale
    G, P, C = SSM_GROUPS, SSM_STATE, SSM_GROUP
    x = jax.random.normal(ks[0], (BATCH, SEQ, D_MODEL), f32)
    norm_w = 1.0 + nrm(ks[1], (DEPTH, D_MODEL), 0.02)
    w_in = nrm(ks[2], (DEPTH, D_MODEL, D_IN), D_MODEL ** -0.5)
    ssm_a_re = -0.5 + nrm(ks[3], (DEPTH, G, P), 0.01)
    ssm_a_im = math.pi * jnp.arange(P, dtype=f32)[None, None, :] + nrm(ks[4], (DEPTH, G, P), 0.01)
    ssm_log_dt = jax.random.uniform(ks[5], (DEPTH, G), f32, math.log(DT_MIN), math.log(DT_MAX))
    ssm_b_re = nrm(ks[6], (DEPTH, G, P, C), C ** -0.5)
    ssm_b_im = nrm(ks[7], (DEPTH, G, P, C), C ** -0.5)
    ssm_c_re = nrm(ks[8], (DEPTH, G, C, P), P ** -0.5)
    ssm_c_im = nrm(ks[9], (DEPTH, G, C, P), P ** -0.5)
    ssm_d = nrm(ks[10], (DEPTH, SSM_WIDTH), 1.0)
    ssm_glu_w = nrm(ks[11], (DEPTH, SSM_WIDTH, SSM_WIDTH), SSM_WIDTH ** -0.5)
    ssm_glu_b = nrm(ks[12], (DEPTH, SSM_WIDTH), 0.01)
    sg_ln_w = 1.0 + nrm(ks[13], (DEPTH, SG_WIDTH), 0.02)
    sg_ln_b = nrm(ks[14], (DEPTH, SG_WIDTH), 0.02)
    sg_w = nrm(ks[15], (DEPTH, SG_HEADS, SG_CHUNK, SG_CHUNK), SG_CHUNK ** -0.5)
    sg_b = 1.0 + nrm(ks[16], (DEPTH, SG_HEADS, SG_CHUNK), 0.02)
    attn_sinks = nrm(ks[17], (DEPTH, ATT_HEADS), 1.0)
    w_branch_a = nrm(ks[18], (DEPTH, SSM_WIDTH, D_MODEL), SSM_WIDTH ** -0.5)
    w_branch_b = nrm(ks[19], (DEPTH, SG_WIDTH, D_MODEL), SG_WIDTH ** -0.5)
    w_branch_c = nrm(ks[20], (DEPTH, ATT_WIDTH, D_MODEL), ATT_WIDTH ** -0.5)
    w_out = nrm(ks[21], (DEPTH, D_MODEL, D_MODEL), D_MODEL ** -0.5)
    final_norm_w = 1.0 + nrm(ks[22], (D_MODEL,), 0.02)
    return {"x": x, "norm_w": norm_w, "w_in": w_in,
            "ssm_a_re": ssm_a_re, "ssm_a_im": ssm_a_im, "ssm_log_dt": ssm_log_dt,
            "ssm_b_re": ssm_b_re, "ssm_b_im": ssm_b_im, "ssm_c_re": ssm_c_re, "ssm_c_im": ssm_c_im,
            "ssm_d": ssm_d, "ssm_glu_w": ssm_glu_w, "ssm_glu_b": ssm_glu_b,
            "sg_ln_w": sg_ln_w, "sg_ln_b": sg_ln_b, "sg_w": sg_w, "sg_b": sg_b,
            "attn_sinks": attn_sinks,
            "w_branch_a": w_branch_a, "w_branch_b": w_branch_b, "w_branch_c": w_branch_c,
            "w_out": w_out, "final_norm_w": final_norm_w}

def reference(x, norm_w, w_in, ssm_a_re, ssm_a_im, ssm_log_dt, ssm_b_re, ssm_b_im,
              ssm_c_re, ssm_c_im, ssm_d, ssm_glu_w, ssm_glu_b, sg_ln_w, sg_ln_b, sg_w, sg_b,
              attn_sinks, w_branch_a, w_branch_b, w_branch_c, w_out, final_norm_w):
    bsz, L, _ = x.shape
    for l in range(DEPTH):
        h = rmsnorm(x, norm_w[l])
        proj = h @ w_in[l]
        u_a, z_a, u_b, v_b, z_b, q, k, v, z_c, gates = jnp.split(proj, IN_OFFSETS, axis=-1)
        y_a = s5_mixer(u_a, ssm_a_re[l], ssm_a_im[l], ssm_log_dt[l], ssm_b_re[l], ssm_b_im[l],
                       ssm_c_re[l], ssm_c_im[l], ssm_d[l], ssm_glu_w[l], ssm_glu_b[l]) * jax.nn.silu(z_a)
        y_b = spatial_gating(jax.nn.gelu(u_b), jax.nn.gelu(v_b), sg_ln_w[l], sg_ln_b[l],
                             sg_w[l], sg_b[l]) * jax.nn.silu(z_b)
        y_c = sliding_window_attention(q, k, v, attn_sinks[l]) * jax.nn.silu(z_c)
        g = jax.nn.sigmoid(gates.reshape(bsz, L, N_BRANCH, D_MODEL))
        merged = (g[:, :, 0] * (y_a @ w_branch_a[l])
                  + g[:, :, 1] * (y_b @ w_branch_b[l])
                  + g[:, :, 2] * (y_c @ w_branch_c[l]))
        x = x + merged @ w_out[l]
    return rmsnorm(x, final_norm_w)


_drawn_inputs = setup_inputs


def setup_inputs(seed=0):
    import zlib

    import numpy as np

    out = dict(_drawn_inputs(seed))
    spreads = {}
    factors = {'norm_w': 4.205,
     'ssm_a_re': 64.0,
     'ssm_a_im': 24.848,
     'ssm_log_dt': 25.544,
     'ssm_b_re': 35.208,
     'ssm_b_im': 34.872,
     'ssm_c_re': 35.784,
     'ssm_c_im': 34.64,
     'ssm_glu_b': 64.0,
     'sg_ln_w': 24.865,
     'sg_ln_b': 24.746,
     'sg_b': 8.0,
     'attn_sinks': 47.514,
     'final_norm_w': 7.966}
    for name, (base, spread) in spreads.items():
        noise = np.random.default_rng([zlib.crc32(name.encode()), seed]).standard_normal(out[name].shape)
        drawn = base * np.exp(spread * noise) if base else spread * noise
        out[name] = __import__('jax').numpy.asarray(drawn.astype(out[name].dtype))
    for name, factor in factors.items():
        out[name] = (out[name] * factor).astype(out[name].dtype)
    return out
```

```python
import math
from contextlib import ExitStack

import concourse.bass as bass
import numpy as np
from concourse import mybir

F32 = mybir.dt.float32
F32R = mybir.dt.float32r
I32 = mybir.dt.int32
ALU = mybir.AluOpType
ACT = mybir.ActivationFunctionType
AX_X = mybir.AxisListType.X

P = 128
DEPTH, SEQ, D = 2, 256, 2048
TOK = SEQ // P
KC = D // P
WID = D // 2
WC = WID // P
COLS = 512
HEADS, KV_HEADS, HD = 16, 2, 64
SG_HEADS = 8
STATE, GROUP = 64, 16
TILES = WID // GROUP * STATE // P
EPS = 1e-6
SCALE = HD ** -0.5

OFF = {}
_at = 0
for _name, _n in (("u_a", WID), ("z_a", WID), ("u_b", WID), ("v_b", WID), ("z_b", WID), ("q", WID),
                  ("kv", 2 * KV_HEADS * HD), ("z_c", WID), ("gates", 3 * D)):
    OFF[_name] = _at
    _at += _n
D_IN = _at


def plan():
    panels, pieces, start = [], [], {}

    def panel(kind, i, weight, chunks, col, cols=COLS):
        start[kind, i] = len(pieces)
        per = 2 * COLS // cols
        for c in range(0, chunks, per):
            pieces.append((weight, c, per, col, cols, kind, i, c + per == chunks))
        if kind != "kv":
            panels.append((kind, i))

    def pair(kind):
        for i in range(2):
            panel(kind, i, "w_in", KC, OFF[kind] + COLS * i)

    def branch(name, n):
        for j in range(D // COLS):
            panel("gate_" + name, j, "w_in", KC, OFF["gates"] + n * D + COLS * j)
            panel("out_" + name, j, "w_branch_" + name, WC, COLS * j)

    pair("u_a"), pair("v_b"), pair("u_b"), pair("z_b"), pair("q")
    panel("kv", 0, "w_in", KC, OFF["kv"], 2 * KV_HEADS * HD)
    branch("b", 1)
    pair("z_c")
    branch("c", 2)
    pair("z_a")
    panel("glu", 0, "glu", WC, 0), panel("glu", 1, "glu", WC, COLS)
    branch("a", 0)
    for j in range(D // COLS):
        panel("w_out", j, "w_out", KC, COLS * j)
    return panels, pieces, start


PANELS, PIECES, START = plan()
NP, NPAN = len(PIECES), len(PANELS)
PAN = {key: n for n, key in enumerate(PANELS)}
END = {}
for _g, _p in enumerate(PIECES):
    if _p[7]:
        END[_p[5], _p[6]] = _g
RAW, RING = 6, 3
assert NP % RAW == 0 and NP % RING == 0 and NPAN % 2 == 0

S5_AT = START["z_b", 0]
GROUPS = []
for _h in (0, 8):
    GROUPS += [(0, _h + i, 4) for i in range(2)] + [(1, _h + 4 * (i // 2) + i % 2, 2) for i in range(4)]
ATT_AT, ATT_STEP = START["out_b", 0] + 4, 3
SCORES_AT, PT_AT, AV_AT = 0, 4, 7


def aux_plan():
    jobs = {}

    def put(g, *job):
        jobs.setdefault(g, []).append(job)

    mix = END["u_b", 1] + 5
    for i in range(4):
        put(mix + i, "mix", i)
    for i in range(4):
        put(END["z_b", i // 2] + 6 + i % 2, "yT", "b", i)
    for i in range(4):
        put(END["kv", 0] + 8 + i // 2, "qT", i)
    put(END["kv", 0] + 10, "kT")
    last = ATT_AT + ATT_STEP * (len(GROUPS) - 1)
    for g in range(ATT_AT, last + AV_AT + 1):
        for what, at in (("pT", PT_AT), ("av", AV_AT), ("scores", SCORES_AT)):
            i, off = divmod(g - ATT_AT - at, ATT_STEP)
            if off == 0 and 0 <= i < len(GROUPS):
                put(g, what, i)
    for i in range(4):
        put(END["z_c", i // 2] + 5 + i % 2, "yT", "c", i)
    for i in range(6):
        put(END["gate_a", 3] + 1 + i // 2, "mT", i)
    for i in range(6, 8):
        put(END["out_a", 3] + 4, "mT", i)
    return jobs


AUX_AFTER = aux_plan()
AUX = [("rstd", 0), ("rstd", 1)]
for _g in sorted(AUX_AFTER):
    for _job in AUX_AFTER[_g]:
        if _job[0] == "qT" and _job[1] == 0:
            AUX.append(("kv",))
        AUX.append(_job)
AUX += [("xT", i) for i in range(8)]
AUXN = {job: n for n, job in enumerate(AUX)}
NAUX, NXT = len(AUX), 8
assert NAUX % 2 == 0 and len(AUXN) == NAUX

DVE_STEPS, ACT_STEPS, POOL_STEPS, RAW_USES = 480, 61, 282, 16 * NP // RAW
GATE_USES = [k for k in PANELS if k[0] in ("z_b", "z_c", "glu") or k[0].startswith("gate")]
GATE_USE = {k: n for n, k in enumerate(GATE_USES)}


class Signal:

    def __init__(self, sem, per_layer=0, start=0):
        self.sem, self.per_layer, self.start = sem, per_layer, start

    def at(self, layer, n):
        return n if layer is None else layer * self.per_layer + (self.start + n)


class Steps:

    def __init__(self, event, layer=None):
        self.sem, self.event, self.layer, self.n = event.sem, event, layer, 0

    def one(self):
        self.n += 1
        return self.sem

    def so_far(self):
        return self.event.at(self.layer, self.n)


def build(nc, x, w, x_first_norm, bT, cT, s5_par, cols, ln_rows, wsT, consts, final_row, out):
    ctx = ExitStack()
    xs = nc.dram_tensor("residual", [DEPTH + 1, SEQ, D], F32, kind="Internal").ap()
    with ctx:
        def sb(name, shape, dt=F32):
            return ctx.enter_context(nc.sbuf_tensor(name, shape, dt))

        def sig(name, per_layer=0, start=0):
            return Signal(ctx.enter_context(nc.semaphore(name)), per_layer, start)

        raw = sb("raw", [P, RAW, 2 * COLS])
        w_hi = sb("w_hi", [P, RING, 2 * COLS], F32R)
        w_lo = sb("w_lo", [P, RING, 2 * COLS], F32R)
        h_hi = sb("h_hi", [P, KC, SEQ], F32R)
        h_lo = sb("h_lo", [P, KC, SEQ], F32R)
        y_hi = sb("y_hi", [P, WC, SEQ], F32R)
        y_lo = sb("y_lo", [P, WC, SEQ], F32R)
        wide = sb("wide", [P, TOK, D])
        v_b, u_b = (wide[:, :, :].rearrange("p t (b n) -> p b t n", b=2)[:, b] for b in range(2))
        gate = sb("gate", [P, TOK, COLS])
        att = sb("att", [P, 5632])
        q = att[:, 0:2048].rearrange("p (t n) -> p t n", t=TOK)
        kv = att[:, 2048:2560].rearrange("p (t n) -> p t n", t=TOK)
        kk = att[:, 2560:3072].rearrange("p (t g n) -> p t g n", t=TOK, g=KV_HEADS)
        qT = att[:, 3072:5120].rearrange("p (c n) -> p c n", c=8)
        kT = att[:, 5120:5632].rearrange("p (g n) -> p g n", g=KV_HEADS)
        ln_w, ln_b = att[:, 0:1024], att[:, 1024:2048]
        ws = att[:, 2048:3072].rearrange("p (h t) -> p h t", h=SG_HEADS)
        par = att[:, 3072:3072 + 96].rearrange("p (k j) -> p k j", k=3)
        scr = att[:, 3200:3200 + 640].rearrange("p (k j) -> p k j", k=20)
        z_a = att[:, 0:2048].rearrange("p (c n) -> p c n", c=WC)
        x_old = att[:, 0:4096].rearrange("p (t n) -> p t n", t=TOK)
        fin = att[:, 0:2048]
        prob = sb("prob", [P, 2, 512])
        probT = sb("probT", [P, 2, 512])
        soft = sb("soft", [P, 5, 3, 4])
        u_a = sb("u_a", [P, WC, SEQ])
        s5b = sb("s5b", [P, 2, WC, P])
        s5c = sb("s5c", [P, 2, WC, P])
        powers = sb("powers", [P, 2, 2, TILES, 16])
        step_par = sb("step_par", [P, 5, TILES])
        turn = sb("turn", [P, 2, 2, SEQ])
        pool_tmp = sb("pool_tmp", [P, 4, SEQ])
        prod = sb("prod", [P, 2, 2, SEQ])
        drive = sb("drive", [P, 2, SEQ])
        scan = sb("scan", [P, 2, SEQ])
        state = sb("state", [P, 2, 2, SEQ])
        con = sb("con", [P, 128 + 256 + 32])
        ident, mask = con[:, 0:128], con[:, 128:384]
        cos, sin = (con[:, 384 + 16 * i:400 + 16 * i].rearrange("p (t k) -> p t k", t=TOK) for i in range(2))
        ones = sb("ones", [P, P])
        col = sb("col", [P, 56])
        c_d, c_glu, c_norm, c_sgb, c_sink = (col[:, a:b] for a, b in
                                             ((0, 8), (8, 16), (16, 32), (32, 40), (40, 56)))
        first_norm = sb("first_norm", [P, KC])
        ssq = sb("ssq", [P, TOK, 4])
        rstd = sb("rstd", [P, TOK])
        nwt = sb("nwt", [P, 6, TOK])
        nwt_i = sb("nwt_i", [P, 2, TOK], I32)
        two_k = sb("two_k", [P, TILES], I32)
        stats = sb("stats", [P, TOK, 2, 6])
        mv = sb("mv", [P, TOK, 2])
        ln_rs = sb("ln_rs", [P, TOK])
        diag = sb("diag", [P, TOK, P])
        rstd_bc = sb("rstd_bc", [P, SEQ])

        acc = [ctx.enter_context(nc.psum_tensor(f"acc{i}", [P, 512], F32)) for i in range(4)]
        bu = ctx.enter_context(nc.psum_tensor("bu", [P, 512], F32))
        ya = ctx.enter_context(nc.psum_tensor("ya", [P, 512], F32))
        side = [ctx.enter_context(nc.psum_tensor(f"side{i}", [P, 512], F32)) for i in range(2)]

        landed = [sig(f"landed{i}", RAW_USES) for i in range(RAW)]
        hi_ready = sig("hi_ready", NP)
        lo_ready = sig("lo_ready", NP)
        piece_done = sig("piece_done", NP, RING)
        taken = [sig(f"taken{i}", NPAN // 2, 1) for i in range(2)]
        aux_done = sig("aux_done", NAUX, NXT)
        aux_taken = [sig(f"aux_taken{i}", NAUX // 2, NXT // 2) for i in range(2)]
        x_ready = sig("x_ready", 4, 4)
        ssq_ready = sig("ssq_ready", 8, 8)
        xt_hi = sig("xt_hi", 2 * NXT, 2 * NXT)
        diag_ready = sig("diag_ready", 2)
        part_hi = sig("part_hi", 16)
        gate_used = sig("gate_used", len(GATE_USES), 1)
        v_ready = sig("v_ready", TOK)
        rope_ready = sig("rope_ready", 1)
        max_ready = sig("max_ready", len(GROUPS))
        p_ready = sig("p_ready", len(GROUPS))
        za_ready = sig("za_ready", 2)
        yg_hi = sig("yg_hi", 4)
        yg_lo = sig("yg_lo", 4)
        ya_ready = sig("ya_ready", 2)
        ya_hi = sig("ya_hi", 2)
        s5_par_ready = sig("s5_par_ready", 1)
        c_scaled = sig("c_scaled", 1)
        turn_ready = sig("turn_ready", TILES)
        turn_used = sig("turn_used", TILES, 2)
        bu_done = sig("bu_done", TILES)
        bu_read = sig("bu_read", TILES, 1)
        state_ready = sig("state_ready", TILES)
        state_used = sig("state_used", TILES, 2)
        y_read = sig("y_read", WC, 1)
        y_act = sig("y_act", WC)
        small_loaded = sig("small_loaded", 16 * 6)
        ws_masked = sig("ws_masked", 1)
        xold_loaded = sig("xold_loaded", 16, 16)
        x_stored = sig("x_stored", 64, 64)
        con_loaded = sig("con_loaded")
        dve_set = sig("dve_set")
        alone = sig("alone")
        dve_step = sig("dve_step", DVE_STEPS)
        act_step = sig("act_step", ACT_STEPS)
        pool_step = sig("pool_step", POOL_STEPS)
        fin_ready = sig("fin_ready")
        stored = sig("stored")

        def accs(n):
            return acc[2 * (n % 2)], acc[2 * (n % 2) + 1]

        def is_channel_major(kind):
            return kind in ("u_a", "z_a", "glu")

        block = ctx.enter_context(nc.Block())

        @block.sync
        def _(sp):
            def load(g, layer):
                weight, c, n, at, width = PIECES[g][:5]
                src = w[weight][layer, P * c:P * (c + n), at:at + width]
                sp.dma_start(raw[:, g % RAW, 0:n * width].rearrange("p (c n) -> p c n", c=n),
                             src.rearrange("(c p) n -> p c n", p=P)).then_inc(landed[g % RAW].sem, 16)

            for g in range(RAW):
                load(g, 0)
            with sp.Fori(0, DEPTH) as l:
                following = 1 - l
                for g in range(NP):
                    sp.wait_ge(lo_ready.sem, lo_ready.at(l, g + 1))
                    sp.sem_inc(alone.sem, 1)
                    load((g + RAW) % NP, l if g + RAW < NP else following)
            for s in landed:
                sp.wait_ge(s.sem, DEPTH * RAW_USES + 16)
            sp.wait_ge(fin_ready.sem, 2)
            sp.dma_start(out.rearrange("(t p) n -> p t n", p=P), wide[:, :, :]).then_inc(stored.sem, 16)
            sp.wait_ge(stored.sem, 16)

        @block.gpsimd
        def _(pool):
            pool.dma_start(con[:, :], consts).then_inc(con_loaded.sem, 16)
            pool.dma_start(first_norm[:, :], x_first_norm).then_inc(con_loaded.sem, 16)
            pool.dma_start(x_old, x.rearrange("(t p) n -> p t n", p=P)).then_inc(xold_loaded.sem, 16)

            def store_x(l, slot):
                for j in range(4):
                    pool.wait_ge(x_ready.sem, x_ready.at(l, j + 1))
                    pool.dma_start(xs[slot, :, COLS * j:COLS * (j + 1)].rearrange("(t p) n -> p t n", p=P),
                                   wide[:, :, COLS * j:COLS * (j + 1)]).then_inc(x_stored.sem, 16)

            store_x(None, 0)
            pool.wait_ge(dve_set.sem, 2)

            with pool.Fori(0, DEPTH) as l:
                st = Steps(pool_step, l)

                pool.wait_ge(x_ready.sem, x_ready.at(l, 0))
                pool.dma_start(par, s5_par[l].rearrange("p (k j) -> p k j", k=3)).then_inc(small_loaded.sem, 16)
                pool.wait_ge(xt_hi.sem, xt_hi.at(l, 0))
                pool.wait_ge(aux_taken[0].sem, aux_taken[0].at(l, 0))
                pool.wait_ge(aux_taken[1].sem, aux_taken[1].at(l, 0))
                pool.dma_start(col[:, :], cols[l]).then_inc(small_loaded.sem, 16)
                pool.dma_start(s5b[:, :, :, :], bT[l]).then_inc(small_loaded.sem, 16)
                pool.dma_start(s5c[:, :, :, :], cT[l]).then_inc(small_loaded.sem, 16)
                pool.dma_start(att[:, 0:2048], ln_rows[l].broadcast_to([P, 2048])).then_inc(small_loaded.sem, 16)
                pool.dma_start(ws, wsT[l]).then_inc(small_loaded.sem, 16)
                pool.wait_ge(small_loaded.sem, small_loaded.at(l, 96))
                pool.sem_inc(alone.sem, 1)
                pool.affine_select(out=ws, in_=ws, compare_op=ALU.is_ge, fill=0.0, base=0,
                                   pattern=[[0, SG_HEADS], [1, P]], channel_multiplier=-1)\
                    .then_inc(ws_masked.sem, 1)

                pool.wait_ge(s5_par_ready.sem, s5_par_ready.at(l, 1))
                pool.sem_inc(alone.sem, 1)
                tmp = pool_tmp[:, :, :].rearrange("p k n -> p (k n)")
                wc, wsn = tmp[:, 0:TILES], tmp[:, TILES:2 * TILES]
                pool.tensor_copy(wc, step_par[:, 1, :]).then_inc(st.one(), 1)
                pool.tensor_copy(wsn, step_par[:, 2, :]).then_inc(st.one(), 1)
                for part in (1, 0):
                    pool.wait_ge(st.sem, st.so_far())
                    pool.sem_inc(alone.sem, 1)
                    tab_c, tab_s = powers[:, part, 0], powers[:, part, 1]
                    pool.memset(tab_c[:, :, 0:1], 1.0).then_inc(st.one(), 1)
                    pool.memset(tab_s[:, :, 0:1], 0.0).then_inc(st.one(), 1)
                    for k in (1, 2, 4, 8):
                        bc = wc.rearrange("p (j o) -> p j o", o=1).broadcast_to([P, TILES, k])
                        bs = wsn.rearrange("p (j o) -> p j o", o=1).broadcast_to([P, TILES, k])
                        t1 = tmp[:, 256:256 + TILES * k].rearrange("p (j k) -> p j k", k=k)
                        t2 = tmp[:, 512:512 + TILES * k].rearrange("p (j k) -> p j k", k=k)
                        oc, os_ = tab_c[:, :, 0:k], tab_s[:, :, 0:k]
                        nc_, ns_ = tab_c[:, :, k:2 * k], tab_s[:, :, k:2 * k]
                        pool.wait_ge(st.sem, st.so_far())
                        pool.tensor_tensor(t1, oc, bc, ALU.mult).then_inc(st.one(), 1)
                        pool.tensor_tensor(t2, os_, bs, ALU.mult).then_inc(st.one(), 1)
                        pool.wait_ge(st.sem, st.so_far())
                        pool.tensor_tensor(nc_, t1, t2, ALU.subtract).then_inc(st.one(), 1)
                        pool.wait_ge(st.sem, st.so_far())
                        pool.tensor_tensor(t1, oc, bs, ALU.mult).then_inc(st.one(), 1)
                        pool.tensor_tensor(t2, os_, bc, ALU.mult).then_inc(st.one(), 1)
                        pool.wait_ge(st.sem, st.so_far())
                        pool.tensor_tensor(ns_, t1, t2, ALU.add).then_inc(st.one(), 1)
                        c2, s2, cs = (tmp[:, 768 + TILES * i:768 + TILES * (i + 1)] for i in range(3))
                        pool.tensor_tensor(c2, wc, wc, ALU.mult).then_inc(st.one(), 1)
                        pool.tensor_tensor(s2, wsn, wsn, ALU.mult).then_inc(st.one(), 1)
                        pool.tensor_tensor(cs, wc, wsn, ALU.mult).then_inc(st.one(), 1)
                        pool.wait_ge(st.sem, st.so_far())
                        pool.tensor_tensor(wc, c2, s2, ALU.subtract).then_inc(st.one(), 1)
                        pool.tensor_tensor(wsn, cs, cs, ALU.add).then_inc(st.one(), 1)
                pool.wait_ge(st.sem, st.so_far())

                def scale_c():
                    kr, ki = step_par[:, 3, :], step_par[:, 4, :]
                    for i in range(0, WC, 2):
                        js = slice(4 * i, 4 * i + 8)
                        kr_b = kr[:, js].rearrange("p (j o) -> p j o", o=1).broadcast_to([P, 8, 32])
                        ki_b = ki[:, js].rearrange("p (j o) -> p j o", o=1).broadcast_to([P, 8, 32])
                        cr = s5c[:, 0, i:i + 2, :].rearrange("p i (j c) -> p (i j) c", c=32)
                        ci = s5c[:, 1, i:i + 2, :].rearrange("p i (j c) -> p (i j) c", c=32)
                        t = [pool_tmp[:, k, :].rearrange("p (j c) -> p j c", c=32) for k in range(4)]
                        pool.tensor_tensor(t[0], cr, kr_b, ALU.mult).then_inc(st.one(), 1)
                        pool.tensor_tensor(t[1], ci, ki_b, ALU.mult).then_inc(st.one(), 1)
                        pool.tensor_tensor(t[2], ci, kr_b, ALU.mult).then_inc(st.one(), 1)
                        pool.tensor_tensor(t[3], cr, ki_b, ALU.mult).then_inc(st.one(), 1)
                        pool.wait_ge(st.sem, st.so_far())
                        pool.tensor_tensor(cr, t[0], t[1], ALU.subtract).then_inc(st.one(), 1)
                        pool.tensor_tensor(t[2], t[2], t[3], ALU.add).then_inc(st.one(), 1)
                        pool.wait_ge(st.sem, st.so_far())
                        pool.sem_inc(alone.sem, 1)
                        pool.tensor_scalar(ci, t[2], -1.0, 0.0, ALU.mult, ALU.add).then_inc(st.one(), 1)
                        pool.wait_ge(st.sem, st.so_far())
                    pool.sem_inc(c_scaled.sem, 1)

                for j in range(TILES):
                    ac, as_ = (powers[:, 0, k, j, :].rearrange("p (a o) -> p a o", o=1).broadcast_to([P, 16, 16])
                               for k in range(2))
                    bc, bs = (powers[:, 1, k, j, :].rearrange("p (o b) -> p o b", o=1).broadcast_to([P, 16, 16])
                              for k in range(2))
                    t = [pool_tmp[:, k, :].rearrange("p (a b) -> p a b", b=16) for k in range(4)]
                    pool.tensor_tensor(t[0], ac, bc, ALU.mult).then_inc(st.one(), 1)
                    pool.tensor_tensor(t[1], as_, bs, ALU.mult).then_inc(st.one(), 1)
                    pool.tensor_tensor(t[2], as_, bc, ALU.mult).then_inc(st.one(), 1)
                    pool.tensor_tensor(t[3], ac, bs, ALU.mult).then_inc(st.one(), 1)
                    pool.wait_ge(st.sem, st.so_far())
                    pool.wait_ge(turn_used.sem, turn_used.at(l, j - 1))
                    tc, ts = (turn[:, j % 2, k, :].rearrange("p (a b) -> p a b", b=16) for k in range(2))
                    pool.tensor_tensor(tc, t[0], t[1], ALU.subtract).then_inc(st.one(), 1)
                    pool.tensor_tensor(ts, t[2], t[3], ALU.add).then_inc(turn_ready.sem, 1)
                    pool.wait_ge(turn_ready.sem, turn_ready.at(l, j + 1))
                    if j == 1:
                        scale_c()
                pool.wait_ge(gate_used.sem, gate_used.at(l, GATE_USE["glu", 1] + 1))
                pool.wait_ge(x_stored.sem, x_stored.at(l, 0))
                pool.dma_start(x_old, xs[l].rearrange("(t p) n -> p t n", p=P)).then_inc(xold_loaded.sem, 16)
                store_x(l, l + 1)
                assert st.n == POOL_STEPS, st.n
            pool.wait_ge(x_ready.sem, 4 * (DEPTH + 1))
            pool.dma_start(fin, final_row.broadcast_to([P, 2048])).then_inc(con_loaded.sem, 16)
            pool.wait_ge(x_stored.sem, 64 * (DEPTH + 1))

        @block.scalar
        def _(act):
            def square_sums(l, st, j):
                act.wait_ge(x_ready.sem, x_ready.at(l, j + 1))
                for t in range(TOK):
                    act.activation(prob[:, t, :], wide[:, t, COLS * j:COLS * (j + 1)], ACT.Square,
                                   accum_out=ssq[:, t, j:j + 1]).then_inc(ssq_ready.sem, 1)
                    act.wait_ge(ssq_ready.sem, ssq_ready.at(l, 2 * j + t + 1))

            def norm_hi(l, m, n, norm):
                act.wait_ge(aux_done.sem, aux_done.at(l, n + 1))
                for c in range(2):
                    act.activation(h_hi[:, 2 * m + c, :], side[n % 2][:, SEQ * c:SEQ * (c + 1)], ACT.Copy,
                                   scale=norm[:, 2 * m + c:2 * m + c + 1]).then_inc(xt_hi.sem, 1)

            act.wait_ge(con_loaded.sem, 32)
            for j in range(4):
                square_sums(None, None, j)
                for m in (2 * j, 2 * j + 1):
                    norm_hi(None, m, m, first_norm)

            with act.Fori(0, DEPTH) as l:
                st = Steps(act_step, l)

                def split(g):
                    _, _, n, _, width = PIECES[g][:5]
                    act.wait_ge(landed[g % RAW].sem, landed[g % RAW].at(l, 16 * (g // RAW + 1)))
                    act.wait_ge(piece_done.sem, piece_done.at(l, g + 1 - RING))
                    act.activation(w_hi[:, g % RING, :], raw[:, g % RAW, :], ACT.Copy).then_inc(hi_ready.sem, 1)

                def by_token(kind, i, func, dst):
                    n = PAN[kind, i]
                    act.wait_ge(piece_done.sem, piece_done.at(l, END[kind, i] + 1))
                    act.activation(dst[0], accs(n)[0][:, :], func, scale=rstd[:, 0:1]).then_inc(st.one(), 1)
                    act.activation(dst[1], accs(n)[1][:, :], func, scale=rstd[:, 1:2])\
                        .then_inc(taken[n % 2].sem, 1)

                def halves(t, i):
                    return [t[:, k, COLS * i:COLS * (i + 1)] for k in range(TOK)]

                def side_hi(job, dst):
                    n = AUXN[job]
                    act.wait_ge(aux_done.sem, aux_done.at(l, n + 1))
                    act.activation(dst, side[n % 2][:, :].rearrange("p (c n) -> p c n", c=2), ACT.Copy)\
                        .then_inc(part_hi.sem, 1)

                def side_copy(job, dst):
                    n = AUXN[job]
                    act.wait_ge(aux_done.sem, aux_done.at(l, n + 1))
                    act.activation(dst, side[n % 2][:, :], ACT.Copy).then_inc(aux_taken[n % 2].sem, 1)

                def exps(i):
                    tile, h0, nh = GROUPS[i]
                    b, keys = i % 2, P * (tile + 1)
                    act.wait_ge(max_ready.sem, max_ready.at(l, i + 1))
                    for k in range(nh):
                        pr = prob[:, b, keys * k:keys * (k + 1)]
                        act.activation(pr, pr, ACT.Exp, bias=soft[:, 1, i % 3, k:k + 1],
                                           accum_out=soft[:, 3, i % 3, k:k + 1]).then_inc(st.one(), 1)
                    act.activation(soft[:, 4, i % 3, 0:nh], soft[:, 2, i % 3, 0:nh], ACT.Exp).then_inc(p_ready.sem, 1)

                act.wait_ge(diag_ready.sem, diag_ready.at(l, 2))
                act.wait_ge(small_loaded.sem, small_loaded.at(l, 96))
                for g in range(NP):
                    split(g)
                    for kind, func, dst in (("v_b", ACT.Gelu_apprx_tanh, v_b), ("u_b", ACT.Gelu_apprx_tanh, u_b),
                                            ("q", ACT.Copy, q)):
                        for i in range(2):
                            if g == END[kind, i] + RING:
                                if kind == "v_b" and i == 0:
                                    act.wait_ge(x_stored.sem, x_stored.at(l, 0))
                                if kind == "q":
                                    act.wait_ge(aux_taken[1].sem, aux_taken[1].at(l, (AUXN["mix", 3] + 1) // 2))
                                    act.wait_ge(aux_taken[0].sem, aux_taken[0].at(l, (AUXN["mix", 3] + 1) // 2))
                                by_token(kind, i, func, halves(dst, i))
                    for kind, i in GATE_USES:
                        if kind != "glu" and g == END[kind, i] + RING:
                            act.wait_ge(gate_used.sem, gate_used.at(l, GATE_USE[kind, i]))
                            by_token(kind, i, ACT.Silu if kind[0] == "z" else ACT.Sigmoid,
                                     [gate[:, k, :] for k in range(TOK)])
                    if g == END["kv", 0] + RING:
                        n = AUXN["kv",]
                        act.wait_ge(aux_done.sem, aux_done.at(l, n + 1))
                        act.activation(kv[:, 0, :], side[n % 2][:, 0:256], ACT.Copy, scale=rstd[:, 0:1]).then_inc(st.one(), 1)
                        act.activation(kv[:, 1, :], side[n % 2][:, 256:512], ACT.Copy, scale=rstd[:, 1:2])\
                            .then_inc(aux_taken[n % 2].sem, 1)
                    for job in AUX_AFTER.get(g - 2, ()):
                        if job[0] == "yT":
                            side_hi(job, y_hi[:, 2 * job[2]:2 * job[2] + 2, :])
                        if job[0] == "mT":
                            side_hi(job, h_hi[:, 2 * job[1]:2 * job[1] + 2, :])
                        if job[0] == "qT":
                            side_copy(job, qT[:, 2 * job[1]:2 * job[1] + 2, :].rearrange("p c n -> p (c n)"))
                        if job[0] == "kT":
                            side_copy(job, kT.rearrange("p g n -> p (g n)"))
                        if job[0] == "pT":
                            side_copy(job, probT[:, job[1] % 2, :])
                    i, off = divmod(g - ATT_AT - 3, ATT_STEP)
                    if off == 0 and 0 <= i < len(GROUPS):
                        exps(i)
                    i, off = divmod(g - S5_AT - 26, 16)
                    if off == 0 and 0 <= i < WC:
                        act.wait_ge(y_read.sem, y_read.at(l, i + 1))
                        act.activation(u_a[:, i, :], u_a[:, i, :], ACT.Gelu_apprx_tanh).then_inc(y_act.sem, 1)
                    for i in range(2):
                        if g == END["z_a", i] + RING + 1:
                            act.wait_ge(taken[PAN["z_a", i] % 2].sem, taken[PAN["z_a", i] % 2].at(l, PAN["z_a", i] // 2 + 1))
                            za = z_a[:, 4 * i:4 * i + 4, :]
                            act.activation(za, za, ACT.Silu).then_inc(za_ready.sem, 1)
                    for i in range(4):
                        if g == END["out_c", 3] + RING + 1 + i:
                            act.wait_ge(y_act.sem, y_act.at(l, WC))
                            act.activation(y_hi[:, 2 * i:2 * i + 2, :], u_a[:, 2 * i:2 * i + 2, :], ACT.Copy)\
                                .then_inc(yg_hi.sem, 1)

                    def glu_gate(i):
                        n = PAN["glu", i]
                        act.wait_ge(gate_used.sem, gate_used.at(l, GATE_USE["glu", i]))
                        act.wait_ge(piece_done.sem, piece_done.at(l, END["glu", i] + 1))
                        g4 = gate[:, :, :].rearrange("p t (c n) -> p (t c) n", n=SEQ)
                        for c in range(4):
                            ins = act.activation(g4[:, c, :], accs(n)[c // 2][:, SEQ * (c % 2):SEQ * (c % 2 + 1)],
                                                 ACT.Sigmoid, bias=c_glu[:, 4 * i + c:4 * i + c + 1])
                            if c < 3:
                                ins.then_inc(st.one(), 1)
                        ins.then_inc(taken[n % 2].sem, 1)

                    def ya_high(i):
                        act.wait_ge(ya_ready.sem, ya_ready.at(l, i + 1))
                        act.wait_ge(piece_done.sem, piece_done.at(l, END["glu", 1] + 1))
                        act.activation(y_hi[:, 4 * i:4 * i + 4, :],
                                       gate[:, :, :].rearrange("p t (c n) -> p (t c) n", n=SEQ), ACT.Copy)\
                            .then_inc(ya_hi.sem, 1)

                    if g == END["glu", 0] + RING:
                        glu_gate(0)
                    if g == END["glu", 1] + RING:
                        ya_high(0)
                        glu_gate(1)
                    if g == END["glu", 1] + RING + 2:
                        ya_high(1)
                    for j in range(3):
                        if g == END["w_out", j] + RING:
                            square_sums(l, st, j)
                square_sums(l, st, 3)
                for m in range(NXT):
                    norm_hi(l, m, AUXN["xT", m], c_norm)
                assert st.n == ACT_STEPS, st.n

        @block.vector
        def _(dve):
            def new_x(l, st, j, n=None):
                if n is not None:
                    dve.wait_ge(piece_done.sem, piece_done.at(l, END["w_out", j] + 1))
                for t in range(TOK):
                    at = slice(COLS * j, COLS * (j + 1))
                    if n is None:
                        dve.tensor_copy(wide[:, t, at], x_old[:, t, at]).then_inc(st.one(), 1)
                    else:
                        ins = dve.tensor_tensor(wide[:, t, at], accs(n)[t][:, :], x_old[:, t, at], ALU.add)
                        if t == 0:
                            ins.then_inc(st.one(), 1)
                        else:
                            ins.then_inc(taken[n % 2].sem, 1)
                if n is None:
                    dve.wait_ge(st.sem, st.so_far())
                else:
                    dve.wait_ge(taken[n % 2].sem, taken[n % 2].at(l, n // 2 + 1))
                dve.sem_inc(x_ready.sem, 1)

            def norm_lo(l, st, m, n, norm):
                dve.wait_ge(xt_hi.sem, xt_hi.at(l, 2 * m + 2))
                for c in range(2):
                    ins = dve.scalar_tensor_tensor(
                        h_lo[:, 2 * m + c, :], side[n % 2][:, SEQ * c:SEQ * (c + 1)],
                        norm[:, 2 * m + c:2 * m + c + 1], h_hi[:, 2 * m + c, :].bitcast(F32),
                        ALU.mult, ALU.subtract)
                    if c == 0:
                        ins.then_inc(st.one(), 1)
                ins.then_inc(aux_taken[n % 2].sem, 1)

            def rsqrt(st, dst, src):
                dve.tensor_copy(nwt[:, 0, :], src).then_inc(st.one(), 1)
                dve.wait_ge(st.sem, st.so_far())
                dve.tensor_scalar(nwt_i[:, 0, :], nwt[:, 0, :].bitcast(I32), 1, None, ALU.logical_shift_right).then_inc(st.one(), 1)
                dve.wait_ge(st.sem, st.so_far())
                dve.tensor_scalar(nwt_i[:, 1, :], nwt_i[:, 0, :], -1.0, float(0x5F3759DF), ALU.mult, ALU.add).then_inc(st.one(), 1)
                dve.wait_ge(st.sem, st.so_far())
                y = nwt_i[:, 1, :].bitcast(F32)
                for k in range(4):
                    dve.tensor_tensor(nwt[:, 1, :], y, y, ALU.mult).then_inc(st.one(), 1)
                    dve.wait_ge(st.sem, st.so_far())
                    dve.tensor_tensor(nwt[:, 2, :], nwt[:, 1, :], nwt[:, 0, :], ALU.mult).then_inc(st.one(), 1)
                    dve.wait_ge(st.sem, st.so_far())
                    dve.tensor_scalar(nwt[:, 3, :], nwt[:, 2, :], -0.5, 1.5, ALU.mult, ALU.add).then_inc(st.one(), 1)
                    dve.wait_ge(st.sem, st.so_far())
                    to = dst if k == 3 else nwt[:, 4 + k % 2, :]
                    dve.tensor_tensor(to, y, nwt[:, 3, :], ALU.mult).then_inc(st.one(), 1)
                    dve.wait_ge(st.sem, st.so_far())
                    y = to

            def row_rstd(l, st):
                dve.wait_ge(ssq_ready.sem, ssq_ready.at(l, 0))
                dve.tensor_reduce(nwt[:, 5, :], ssq[:, :, :], AX_X, ALU.add).then_inc(st.one(), 1)
                dve.wait_ge(st.sem, st.so_far())
                dve.tensor_scalar(nwt[:, 5, :], nwt[:, 5, :], 1.0 / D, EPS, ALU.mult, ALU.add).then_inc(st.one(), 1)
                dve.wait_ge(st.sem, st.so_far())
                rsqrt(st, rstd[:, :], nwt[:, 5, :])

            dve.memset(ones[:, :], 1.0).then_inc(dve_set.sem, 1)
            dve.memset(nwt[:, :, :], 0.0).then_inc(dve_set.sem, 1)
            dve.sem_inc(gate_used.sem, 1)
            dve.sem_inc(turn_used.sem, 2)
            dve.sem_inc(bu_read.sem, 1)
            dve.sem_inc(y_read.sem, 1)
            first = Steps(sig("dve_first_step"))

            dve.wait_ge(con_loaded.sem, 32)
            dve.wait_ge(xold_loaded.sem, 16)
            dve.wait_ge(dve_set.sem, 2)
            for j in range(4):
                new_x(None, first, j)
                for m in (2 * j, 2 * j + 1):
                    norm_lo(None, first, m, m, first_norm)

            with dve.Fori(0, DEPTH) as l:
                st = Steps(dve_step, l)

                def split(g):
                    dve.wait_ge(hi_ready.sem, hi_ready.at(l, g + 1))
                    dve.tensor_tensor(w_lo[:, g % RING, :], raw[:, g % RAW, :], w_hi[:, g % RING, :].bitcast(F32),
                                      ALU.subtract).then_inc(lo_ready.sem, 1)

                def was_taken(kind, i):
                    dve.wait_ge(taken[PAN[kind, i] % 2].sem, taken[PAN[kind, i] % 2].at(l, PAN[kind, i] // 2 + 1))

                def by_channel(kind, i, dst):
                    n = PAN[kind, i]
                    dve.wait_ge(piece_done.sem, piece_done.at(l, END[kind, i] + 1))
                    for b in range(2):
                        ins = dve.tensor_tensor(
                            dst[:, 4 * i + 2 * b:4 * i + 2 * b + 2, :],
                            accs(n)[b][:, :].rearrange("p (c n) -> p c n", c=2),
                            rstd_bc[:, :].rearrange("p (o n) -> p o n", o=1).broadcast_to([P, 2, SEQ]), ALU.mult)
                        if b == 0:
                            ins.then_inc(st.one(), 1)
                    ins.then_inc(taken[n % 2].sem, 1)

                def s5_parameters():
                    dve.wait_ge(small_loaded.sem, small_loaded.at(l, 96))
                    S = [scr[:, k, :] for k in range(20)]

                    def ts(o, a, s1, s2, op0, op1):
                        dve.tensor_scalar(o, a, s1, s2, op0, op1).then_inc(st.one(), 1), dve.wait_ge(st.sem, st.so_far())

                    def tt(o, a, b, op):
                        dve.tensor_tensor(o, a, b, op).then_inc(st.one(), 1), dve.wait_ge(st.sem, st.so_far())

                    def stt(o, a, s, b, op0, op1):
                        dve.scalar_tensor_tensor(o, a, s, b, op0, op1).then_inc(st.one(), 1), dve.wait_ge(st.sem, st.so_far())

                    magic = 12582912.0

                    def expm1(o, xin, scale_out):
                        xx, k, r, p = S[12:16]
                        ts(xx, xin, -88.02, 88.0, ALU.max, ALU.min)
                        ts(k, xx, 1.0 / math.log(2.0), magic, ALU.mult, ALU.add)
                        ts(k, k, magic, None, ALU.subtract, ALU.bypass)
                        stt(r, k, -0.693359375, xx, ALU.mult, ALU.add)
                        stt(r, k, 2.12194440e-4, r, ALU.mult, ALU.add)
                        ts(p, r, 1.0 / math.factorial(8), None, ALU.mult, ALU.bypass)
                        for n in range(7, 0, -1):
                            stt(p, p, 1.0 / math.factorial(n), r, ALU.add, ALU.mult)
                        ts(two_k[:, :], k, 127.0, 8388608.0, ALU.add, ALU.mult)
                        pw = two_k[:, :].bitcast(F32)
                        tt(p, p, pw, ALU.mult)
                        if scale_out:
                            tt(o, p, pw, ALU.add)
                        else:
                            stt(o, pw, -1.0, p, ALU.add, ALU.add)

                    re, im, log_dt = par[:, 0, :], par[:, 1, :], par[:, 2, :]
                    dt, m, th, k, r, z, z2, s, cm, t = S[0:10]
                    expm1(dt, log_dt, True)
                    yield
                    tt(t, re, dt, ALU.mult)
                    expm1(m, t, False)
                    yield
                    tt(th, im, dt, ALU.mult)
                    ts(k, th, 1.0 / (2 * math.pi), magic, ALU.mult, ALU.add)
                    ts(k, k, magic, None, ALU.subtract, ALU.bypass)
                    p1 = 6.28125
                    p2 = float(np.round((2 * math.pi - p1) * 2.0 ** 20) / 2.0 ** 20)
                    p3 = 2 * math.pi - p1 - p2
                    stt(r, k, -p1, th, ALU.mult, ALU.add)
                    stt(r, k, -p2, r, ALU.mult, ALU.add)
                    stt(r, k, -p3, r, ALU.mult, ALU.add)
                    yield
                    ts(z, r, 0.25, None, ALU.mult, ALU.bypass)
                    tt(z2, z, z, ALU.mult)
                    ts(s, z2, -1.0 / math.factorial(11), None, ALU.mult, ALU.bypass)
                    for n, sign in ((9, 1.0), (7, -1.0), (5, 1.0), (3, -1.0)):
                        stt(s, s, sign / math.factorial(n), z2, ALU.add, ALU.mult)
                    stt(s, s, 1.0, z, ALU.add, ALU.mult)
                    yield
                    ts(cm, z2, 1.0 / math.factorial(12), None, ALU.mult, ALU.bypass)
                    for n, sign in ((10, -1.0), (8, 1.0), (6, -1.0), (4, 1.0), (2, -1.0)):
                        stt(cm, cm, sign / math.factorial(n), z2, ALU.add, ALU.mult)
                    for _ in range(2):
                        yield
                        stt(t, cm, 1.0, s, ALU.add, ALU.mult)
                        tt(cm, s, s, ALU.mult)
                        ts(cm, cm, -2.0, None, ALU.mult, ALU.bypass)
                        ts(s, t, 2.0, None, ALU.mult, ALU.bypass)
                    ts(step_par[:, 0, :], m, 1.0, None, ALU.add, ALU.bypass)
                    ts(step_par[:, 1, :], cm, 1.0, None, ALU.add, ALU.bypass)
                    ts(step_par[:, 2, :], s, 1.0, None, ALU.mult, ALU.bypass)
                    yield
                    l_re, l_im, inv, a, b = S[10], S[11], S[16], S[17], S[18]
                    tt(t, m, cm, ALU.mult)
                    tt(l_re, m, cm, ALU.add)
                    tt(l_re, l_re, t, ALU.add)
                    stt(l_im, m, 1.0, s, ALU.add, ALU.mult)
                    tt(a, re, re, ALU.mult)
                    tt(b, im, im, ALU.mult)
                    tt(a, a, b, ALU.add)
                    dve.reciprocal(inv, a).then_inc(st.one(), 1), dve.wait_ge(st.sem, st.so_far())
                    yield
                    tt(a, l_re, re, ALU.mult)
                    tt(b, l_im, im, ALU.mult)
                    tt(a, a, b, ALU.add)
                    tt(step_par[:, 3, :], a, inv, ALU.mult)
                    tt(a, l_im, re, ALU.mult)
                    tt(b, l_re, im, ALU.mult)
                    tt(a, a, b, ALU.subtract)
                    dve.tensor_tensor(step_par[:, 4, :], a, inv, ALU.mult).then_inc(s5_par_ready.sem, 1)

                def s5_tile(j, stage):
                    tc, ts = (turn[:, j % 2, k, :].rearrange("p (o n) -> p o n", o=1).broadcast_to([P, 2, SEQ])
                              for k in range(2))
                    if stage == 0:
                        dve.wait_ge(turn_ready.sem, turn_ready.at(l, j + 1))
                        dve.wait_ge(bu_done.sem, bu_done.at(l, j + 1))
                        if j > 0:
                            dve.wait_ge(state_ready.sem, state_ready.at(l, j))
                        drv = bu[:, :].rearrange("p (k n) -> p k n", k=2)
                        dve.tensor_tensor(prod[:, 0], drv, tc, ALU.mult).then_inc(st.one(), 1)
                        dve.tensor_tensor(prod[:, 1], drv, ts, ALU.mult).then_inc(bu_read.sem, 1)
                    if stage == 1:
                        dve.wait_ge(bu_read.sem, bu_read.at(l, j + 1))
                        dve.tensor_tensor(drive[:, 0], prod[:, 0, 0], prod[:, 1, 1], ALU.add).then_inc(st.one(), 1)
                        dve.tensor_tensor(drive[:, 1], prod[:, 0, 1], prod[:, 1, 0], ALU.subtract).then_inc(st.one(), 1)
                        dve.wait_ge(st.sem, st.so_far())
                        decay = step_par[:, 0, j:j + 1].broadcast_to([P, SEQ])
                        for k in range(2):
                            dve.tensor_tensor_scan(scan[:, k], decay, drive[:, k], 0.0, ALU.mult, ALU.add).then_inc(st.one(), 1)
                    if stage == 2:
                        dve.wait_ge(st.sem, st.so_far())
                        dve.tensor_tensor(prod[:, 0], scan[:, :, :], tc, ALU.mult).then_inc(st.one(), 1)
                        dve.tensor_tensor(prod[:, 1], scan[:, :, :], ts, ALU.mult).then_inc(turn_used.sem, 1)
                    if stage == 3:
                        dve.wait_ge(st.sem, st.so_far())
                        dve.wait_ge(turn_used.sem, turn_used.at(l, j + 1))
                        dve.wait_ge(state_used.sem, state_used.at(l, j - 1))
                        dve.tensor_tensor(state[:, j % 2, 0], prod[:, 0, 0], prod[:, 1, 1], ALU.subtract).then_inc(st.one(), 1)
                        dve.tensor_tensor(state[:, j % 2, 1], prod[:, 0, 1], prod[:, 1, 0], ALU.add)\
                            .then_inc(state_ready.sem, 1)

                def layer_norm():
                    for t in range(TOK):
                        for i in range(2):
                            dve.bn_stats(stats[:, t, i, :], v_b[:, t, COLS * i:COLS * (i + 1)]).then_inc(st.one(), 1)
                        yield
                    dve.wait_ge(st.sem, st.so_far())
                    dve.sem_inc(alone.sem, 1)
                    for t in range(TOK):
                        dve.bn_aggr(mv[:, t, :], stats[:, t, :, :]).then_inc(st.one(), 1)
                    dve.wait_ge(st.sem, st.so_far())
                    dve.tensor_scalar(ln_rs[:, :], mv[:, :, 1], EPS, None, ALU.add, ALU.bypass).then_inc(st.one(), 1)
                    dve.wait_ge(st.sem, st.so_far())
                    yield
                    rsqrt(st, ln_rs[:, :], ln_rs[:, :])
                    for t in range(TOK):
                        yield
                        dve.scalar_tensor_tensor(v_b[:, t, :], v_b[:, t, :], mv[:, t, 0:1], ln_w,
                                                 ALU.subtract, ALU.mult).then_inc(st.one(), 1)
                    for t in range(TOK):
                        yield
                        dve.wait_ge(st.sem, st.so_far())
                        dve.scalar_tensor_tensor(v_b[:, t, :], v_b[:, t, :], ln_rs[:, t:t + 1], ln_b,
                                                 ALU.mult, ALU.add).then_inc(v_ready.sem, 1)

                def mixed(i):
                    n, t, h0 = AUXN["mix", i], i // 2, 4 * (i % 2)
                    dve.wait_ge(aux_done.sem, aux_done.at(l, n + 1))
                    for h in range(4):
                        at = slice(P * (h0 + h), P * (h0 + h + 1))
                        ins = dve.scalar_tensor_tensor(u_b[:, t, at], side[n % 2][:, P * h:P * (h + 1)],
                                                       c_sgb[:, h0 + h:h0 + h + 1], u_b[:, t, at],
                                                       ALU.add, ALU.mult)
                        if h < 3:
                            ins.then_inc(st.one(), 1)
                    ins.then_inc(aux_taken[n % 2].sem, 1)

                def times_gate(kind, i, dst):
                    was_taken(kind, i)
                    if kind == "z_b":
                        for n in (AUXN["mix", 2], AUXN["mix", 3]):
                            dve.wait_ge(aux_taken[n % 2].sem, aux_taken[n % 2].at(l, n // 2 + 1))
                    for t in range(TOK):
                        at = dst[:, t, COLS * i:COLS * (i + 1)]
                        ins = dve.tensor_tensor(at, at, gate[:, t, :], ALU.mult)
                        if t == 0:
                            ins.then_inc(st.one(), 1)
                    ins.then_inc(gate_used.sem, 1)

                def side_lo(job, dst, hi, nth):
                    n = AUXN[job]
                    dve.wait_ge(part_hi.sem, part_hi.at(l, nth + 1))
                    dve.tensor_tensor(dst, side[n % 2][:, :].rearrange("p (c n) -> p c n", c=2), hi.bitcast(F32),
                                      ALU.subtract).then_inc(aux_taken[n % 2].sem, 1)

                def rotary():
                    dve.wait_ge(aux_taken[AUXN["kv",] % 2].sem, aux_taken[AUXN["kv",] % 2].at(l, AUXN["kv",] // 2 + 1))
                    for src, nh in ((q.rearrange("p t (h d) -> p t h d", d=HD), HEADS),
                                    (kv[:, :, 0:P].rearrange("p t (h d) -> p t h d", d=HD), KV_HEADS)):
                        a, b = src[:, :, :, 0:8], src[:, :, :, 8:16]
                        c, s = (tab.rearrange("p t (o k) -> p t o k", o=1).broadcast_to([P, TOK, nh, 8])
                                for tab in (cos, sin))
                        t = [prob[:, k // 2, 256 * (k % 2):256 * (k % 2) + 16 * nh]
                             .rearrange("p (t h k) -> p t h k", t=TOK, k=8) for k in range(4)]
                        yield
                        dve.tensor_tensor(t[0], a, c, ALU.mult).then_inc(st.one(), 1)
                        dve.tensor_tensor(t[1], b, s, ALU.mult).then_inc(st.one(), 1)
                        dve.tensor_tensor(t[2], b, c, ALU.mult).then_inc(st.one(), 1)
                        dve.tensor_tensor(t[3], a, s, ALU.mult).then_inc(st.one(), 1)
                        dve.wait_ge(st.sem, st.so_far())
                        dve.tensor_tensor(a, t[0], t[1], ALU.subtract).then_inc(st.one(), 1)
                        dve.tensor_tensor(b, t[2], t[3], ALU.add).then_inc(st.one(), 1)
                        dve.wait_ge(st.sem, st.so_far())
                    yield
                    for t in range(TOK):
                        k_src = kv[:, t, 0:P].rearrange("p (g o d) -> p g o d", g=KV_HEADS, o=1)\
                            .broadcast_to([P, KV_HEADS, 2, HD])
                        dve.tensor_copy(kk[:, t, :, :].rearrange("p g (o d) -> p g o d", o=2), k_src).then_inc(st.one(), 1)
                    dve.wait_ge(st.sem, st.so_far())
                    dve.sem_inc(rope_ready.sem, 1)

                def softmax_max(i):
                    tile, h0, nh = GROUPS[i]
                    b, keys, n = i % 2, P * (tile + 1), AUXN["scores", i]
                    dve.wait_ge(aux_done.sem, aux_done.at(l, n + 1))
                    pr = prob[:, b, 0:nh * keys].rearrange("p (h k) -> p h k", h=nh)
                    m = mask[:, 256 - keys:256].rearrange("p (o k) -> p o k", o=1).broadcast_to([P, nh, keys])
                    dve.scalar_tensor_tensor(pr, side[n % 2][:, 0:nh * keys].rearrange("p (h k) -> p h k", h=nh),
                                             SCALE, m, ALU.mult, ALU.add).then_inc(aux_taken[n % 2].sem, 1)
                    dve.wait_ge(aux_taken[n % 2].sem, aux_taken[n % 2].at(l, n // 2 + 1))
                    sinks = c_sink[:, h0:h0 + 2 * nh - 1:2]
                    mx, neg, sk = soft[:, 0, i % 3, 0:nh], soft[:, 1, i % 3, 0:nh], soft[:, 2, i % 3, 0:nh]
                    dve.tensor_reduce(mx, pr, AX_X, ALU.max).then_inc(st.one(), 1)
                    dve.wait_ge(st.sem, st.so_far())
                    dve.tensor_tensor(mx, mx, sinks, ALU.max).then_inc(st.one(), 1)
                    dve.wait_ge(st.sem, st.so_far())
                    dve.tensor_tensor(sk, sinks, mx, ALU.subtract).then_inc(st.one(), 1)
                    dve.tensor_scalar(neg, mx, -1.0, None, ALU.mult, ALU.bypass).then_inc(max_ready.sem, 1)

                def attended(i):
                    tile, h0, nh = GROUPS[i]
                    b, n = i % 2, AUXN["av", i]
                    den = soft[:, 0, i % 3, 0:nh]
                    dve.wait_ge(p_ready.sem, p_ready.at(l, i + 1))
                    dve.tensor_tensor(den, soft[:, 3, i % 3, 0:nh], soft[:, 4, i % 3, 0:nh], ALU.add).then_inc(st.one(), 1)
                    dve.wait_ge(st.sem, st.so_far())
                    dve.reciprocal(soft[:, 2, i % 3, 0:nh], den).then_inc(st.one(), 1)
                    dve.wait_ge(st.sem, st.so_far())
                    dve.wait_ge(aux_done.sem, aux_done.at(l, n + 1))
                    dve.tensor_tensor(
                        q[:, tile, :].rearrange("p (h d) -> p h d", d=HD)[:, h0:h0 + 2 * nh - 1:2, :],
                        side[n % 2][:, 0:nh * HD].rearrange("p (h d) -> p h d", d=HD),
                        soft[:, 2, i % 3, 0:nh].rearrange("p (h o) -> p h o", o=1).broadcast_to([P, nh, HD]),
                        ALU.mult).then_inc(aux_taken[n % 2].sem, 1)

                def merge(name, j):
                    n = PAN["out_" + name, j]
                    dve.wait_ge(piece_done.sem, piece_done.at(l, END["out_" + name, j] + 1))
                    was_taken("gate_" + name, j)
                    for t in range(TOK):
                        at = wide[:, t, COLS * j:COLS * (j + 1)] if name == "b" else gate[:, t, :]
                        ins = dve.tensor_tensor(at, accs(n)[t][:, :], gate[:, t, :], ALU.mult)
                        if t == 0:
                            ins.then_inc(st.one(), 1)
                    ins.then_inc(taken[n % 2].sem, 1)
                    if name == "b":
                        dve.wait_ge(taken[n % 2].sem, taken[n % 2].at(l, n // 2 + 1))
                        dve.sem_inc(gate_used.sem, 1)

                def merge_add(name, j):
                    n = PAN["out_" + name, j]
                    dve.wait_ge(st.sem, st.so_far())
                    dve.wait_ge(taken[n % 2].sem, taken[n % 2].at(l, n // 2 + 1))
                    for t in range(TOK):
                        at = wide[:, t, COLS * j:COLS * (j + 1)]
                        ins = dve.tensor_tensor(at, at, gate[:, t, :], ALU.add)
                        if t == 0:
                            ins.then_inc(st.one(), 1)
                    ins.then_inc(gate_used.sem, 1)

                gate4 = gate[:, :, :].rearrange("p t (c n) -> p (t c) n", n=SEQ)

                def ya_products(i):
                    was_taken("glu", i)
                    dve.wait_ge(za_ready.sem, za_ready.at(l, i + 1))
                    dve.tensor_tensor(gate4, gate4, z_a[:, 4 * i:4 * i + 4, :], ALU.mult).then_inc(st.one(), 1)
                    dve.wait_ge(st.sem, st.so_far())
                    dve.tensor_tensor(gate4, gate4, u_a[:, 4 * i:4 * i + 4, :], ALU.mult).then_inc(ya_ready.sem, 1)

                def ya_low(i):
                    dve.wait_ge(ya_hi.sem, ya_hi.at(l, i + 1))
                    dve.tensor_tensor(y_lo[:, 4 * i:4 * i + 4, :], gate4,
                                      y_hi[:, 4 * i:4 * i + 4, :].bitcast(F32), ALU.subtract)\
                        .then_inc(gate_used.sem, 1)

                row_rstd(l, st)
                for t in range(TOK):
                    dve.tensor_scalar(diag[:, t, :], ident, rstd[:, t:t + 1], None, ALU.mult, ALU.bypass)\
                        .then_inc(diag_ready.sem, 1)

                for g in range(NP):
                    split(g)
                    if g == 1:
                        for t in range(TOK):
                            dve.wait_ge(aux_done.sem, aux_done.at(l, t + 1))
                            dve.tensor_copy(rstd_bc[:, P * t:P * (t + 1)], side[t][:, 0:P])\
                                .then_inc(aux_taken[t].sem, 1)
                    if g == 3:
                        steps = s5_parameters()
                    for i in range(2):
                        if g == END["u_a", i] + RING:
                            if i == 0:
                                dve.wait_ge(aux_taken[0].sem, aux_taken[0].at(l, 1)), dve.wait_ge(aux_taken[1].sem, aux_taken[1].at(l, 1))
                            by_channel("u_a", i, u_a)
                        if g == END["z_b", i] + RING:
                            times_gate("z_b", i, u_b)
                        if g == END["z_c", i] + RING:
                            times_gate("z_c", i, q)
                        if g == END["z_a", i] + RING:
                            by_channel("z_a", i, z_a)
                    if g == END["v_b", 1] + RING + 1:
                        was_taken("v_b", 0), was_taken("v_b", 1)
                        steps = layer_norm()
                    if g == END["kv", 0] + RING:
                        steps = rotary()
                    if g >= 3:
                        next(steps, None)
                    for job in AUX_AFTER.get(g - 2, ()):
                        if job[0] == "mix":
                            if job[1] == 0:
                                was_taken("u_b", 0), was_taken("u_b", 1)
                            mixed(job[1])
                        if job[0] == "yT":
                            m = job[2]
                            side_lo(job, y_lo[:, 2 * m:2 * m + 2, :], y_hi[:, 2 * m:2 * m + 2, :],
                                    m + (4 if job[1] == "c" else 0))
                        if job[0] == "mT":
                            m = job[1]
                            side_lo(job, h_lo[:, 2 * m:2 * m + 2, :], h_hi[:, 2 * m:2 * m + 2, :], 8 + m)
                        if job[0] == "scores":
                            softmax_max(job[1])
                        if job[0] == "av":
                            attended(job[1])
                    k, stage = divmod(g - S5_AT - 3, 4)
                    if 0 <= k < TILES:
                        s5_tile(k, stage)
                    i, off = divmod(g - S5_AT - 21, 16)
                    if off == 0 and 0 <= i < WC:
                        dve.wait_ge(state_used.sem, state_used.at(l, 4 * i + 4))
                        dve.scalar_tensor_tensor(u_a[:, i, :], u_a[:, i, :], c_d[:, i:i + 1], ya[:, 0:SEQ],
                                                 ALU.mult, ALU.add).then_inc(y_read.sem, 1)
                    for name in "bca":
                        for j in range(4):
                            if g == END["out_" + name, j] + RING:
                                merge(name, j)
                            if name != "b" and g == END["out_" + name, j] + RING + 1:
                                merge_add(name, j)
                    for i in range(4):
                        if g == END["out_c", 3] + RING + 1 + i:
                            dve.wait_ge(yg_hi.sem, yg_hi.at(l, i + 1))
                            dve.tensor_tensor(y_lo[:, 2 * i:2 * i + 2, :], u_a[:, 2 * i:2 * i + 2, :],
                                              y_hi[:, 2 * i:2 * i + 2, :].bitcast(F32), ALU.subtract)\
                                .then_inc(yg_lo.sem, 1)
                    if g == END["glu", 0] + RING:
                        ya_products(0)
                    if g == END["glu", 1] + RING:
                        ya_low(0)
                    if g == END["glu", 1] + RING + 1:
                        ya_products(1)
                    if g == END["glu", 1] + RING + 2:
                        ya_low(1)
                    if g == END["w_out", 0] + RING:
                        dve.wait_ge(xold_loaded.sem, xold_loaded.at(l, 16))
                    for j in range(3):
                        if g == END["w_out", j] + RING:
                            new_x(l, st, j, PAN["w_out", j])
                new_x(l, st, 3, PAN["w_out", 3])
                for m in range(NXT):
                    norm_lo(l, st, m, AUXN["xT", m], c_norm)
                assert st.n == DVE_STEPS, st.n

            dve.wait_ge(ssq_ready.sem, 8 * (DEPTH + 1))
            last = Steps(sig("dve_last_step"))
            row_rstd(None, last)
            dve.wait_ge(con_loaded.sem, 48)
            dve.wait_ge(x_stored.sem, 64 * (DEPTH + 1))
            for t in range(TOK):
                dve.scalar_tensor_tensor(wide[:, t, :], wide[:, t, :], rstd[:, t:t + 1], fin,
                                         ALU.mult, ALU.mult).then_inc(fin_ready.sem, 1)

        @block.tensor
        def _(pe):
            def transposes(dst, parts):
                for i, part in enumerate(parts):
                    ins = pe.transpose(dst[:, P * i:P * (i + 1)], part, ident)
                return ins

            def x_transposes(l, m, n):
                pe.wait_ge(x_ready.sem, x_ready.at(l, m // 2 + 1))
                transposes(side[n % 2], [wide[:, t, P * c:P * (c + 1)] for c in (2 * m, 2 * m + 1)
                                         for t in range(TOK)]).then_inc(aux_done.sem, 1)

            pe.sem_inc(piece_done.sem, RING)
            pe.sem_inc(state_used.sem, 2)
            pe.sem_inc(taken[0].sem, 1)
            pe.sem_inc(taken[1].sem, 1)
            pe.wait_ge(con_loaded.sem, 32)
            pe.wait_ge(dve_set.sem, 2)
            for m in range(NXT):
                if m >= 2:
                    pe.wait_ge(aux_taken[m % 2].sem, m // 2)
                x_transposes(None, m, m)

            with pe.Fori(0, DEPTH) as l:

                def side_free(n):
                    pe.wait_ge(aux_taken[n % 2].sem, aux_taken[n % 2].at(l, n // 2))

                def piece(g):
                    _, c0, nch, _, width, kind, i, last = PIECES[g]
                    slot, first = g % RING, c0 == 0
                    if kind == "kv":
                        banks = [side[AUXN["kv",] % 2]]
                    else:
                        n = PAN[kind, i]
                        banks = accs(n)
                    if first:
                        if kind == "kv":
                            side_free(AUXN["kv",])
                        else:
                            pe.wait_ge(taken[n % 2].sem, taken[n % 2].at(l, n // 2))
                    pe.wait_ge(lo_ready.sem, lo_ready.at(l, g + 1))
                    s_hi, s_lo = (y_hi, y_lo) if kind == "glu" or kind[:3] == "out" else (h_hi, h_lo)
                    for c in range(nch):
                        wh, wl = (t[:, slot, width * c:width * (c + 1)] for t in (w_hi, w_lo))
                        k = c0 + c
                        if kind == "w_out" and i == 0 and k % 2 == 0:
                            m = AUXN["mT", k // 2]
                            pe.wait_ge(aux_taken[m % 2].sem, aux_taken[m % 2].at(l, m // 2 + 1))
                        if kind == "u_a" and i == 0 and k % 2 == 0:
                            m = k // 2
                            pe.wait_ge(aux_taken[m % 2].sem, aux_taken[m % 2].at(l, m // 2 + 1 - NXT // 2))
                        if is_channel_major(kind):
                            for f in range(4):
                                o = banks[f // 2][:, SEQ * (f % 2):SEQ * (f % 2 + 1)]
                                at = slice(P * f, P * (f + 1))
                                for r, (a, b) in enumerate(((wh, s_hi), (wh, s_lo), (wl, s_hi))):
                                    ins = pe.matmul(o, a[:, at], b[:, k, :],
                                                    start=first and c == 0 and r == 0 and f % 2 == 0,
                                                    stop=last and c == nch - 1 and r == 2,
                                                    skip_group_check=True)
                        else:
                            for t in range(TOK):
                                o = banks[0][:, width * t:width * (t + 1)] if kind == "kv" else banks[t][:, :]
                                at = slice(P * t, P * (t + 1))
                                for r, (a, b) in enumerate(((s_hi, wh), (s_hi, wl), (s_lo, wh))):
                                    ins = pe.matmul(o, a[:, k, at], b,
                                                    start=first and c == 0 and r == 0 and
                                                    not (kind == "kv" and t == 1),
                                                    stop=last and c == nch - 1 and r == 2,
                                                    skip_group_check=kind == "kv")
                    ins.then_inc(piece_done.sem, 1)
                    if last and kind == "kv":
                        pe.wait_ge(piece_done.sem, piece_done.at(l, g + 1))
                        pe.sem_inc(aux_done.sem, 1)

                def s5_feed(k):
                    at = 32 * (k % 4)
                    pe.wait_ge(bu_read.sem, bu_read.at(l, k))
                    for part in range(2):
                        ins = pe.matmul(bu[:, SEQ * part:SEQ * (part + 1)], s5b[at:at + 32, part, k // 4, :],
                                        u_a[at:at + 32, k // 4, :], start=True, stop=True,
                                        tile_position=(at, 0))
                    ins.then_inc(bu_done.sem, 1)

                def s5_out(k):
                    at = 32 * (k % 4)
                    pe.wait_ge(state_ready.sem, state_ready.at(l, k + 1))
                    if k % 4 == 0:
                        pe.wait_ge(y_read.sem, y_read.at(l, k // 4))
                    for part in range(2):
                        ins = pe.matmul(ya[at:at + 32, 0:SEQ], s5c[:, part, k // 4, at:at + 32],
                                        state[:, k % 2, part, :], start=part == 0, stop=part == 1,
                                        tile_position=(0, at))
                    ins.then_inc(state_used.sem, 1)

                def side_job(job):
                    n = AUXN[job]
                    bank = side[n % 2]
                    what = job[0]
                    if what == "mix":
                        t, h0 = job[1] // 2, 4 * (job[1] % 2)
                        pe.wait_ge(v_ready.sem, v_ready.at(l, TOK)), pe.wait_ge(ws_masked.sem, ws_masked.at(l, 1))
                        side_free(n)
                        for h in range(4):
                            ins = pe.matmul(bank[:, P * h:P * (h + 1)], ws[:, h0 + h, :],
                                            v_b[:, t, P * (h0 + h):P * (h0 + h + 1)], start=True, stop=True)
                    if what in ("yT", "mT"):
                        m = job[-1]
                        if what == "mT":
                            src = wide
                            pe.wait_ge(gate_used.sem, gate_used.at(l, GATE_USE["gate_a", m // 2] + 1))
                        else:
                            src = u_b if job[1] == "b" else q
                            pe.wait_ge(gate_used.sem, gate_used.at(l, GATE_USE["z_" + job[1], m // 2] + 1))
                        side_free(n)
                        ins = transposes(bank, [src[:, t, P * c:P * (c + 1)] for c in (2 * m, 2 * m + 1)
                                                for t in range(TOK)])
                    if what == "qT":
                        pe.wait_ge(rope_ready.sem, rope_ready.at(l, 1))
                        side_free(n)
                        ins = transposes(bank, [q[:, t, P * c:P * (c + 1)] for c in (2 * job[1], 2 * job[1] + 1)
                                                for t in range(TOK)])
                    if what == "kT":
                        side_free(n)
                        ins = transposes(bank, [kk[:, t, g, :] for g in range(KV_HEADS) for t in range(TOK)])
                    if what == "scores":
                        tile, h0, nh = GROUPS[job[1]]
                        keys = P * (tile + 1)
                        if job[1] == 0:
                            m = AUXN["kT",]
                            pe.wait_ge(aux_taken[m % 2].sem, aux_taken[m % 2].at(l, m // 2 + 1))
                            m = AUXN["qT", 3]
                            pe.wait_ge(aux_taken[m % 2].sem, aux_taken[m % 2].at(l, m // 2 + 1))
                        side_free(n)
                        for i in range(nh):
                            h = h0 + 2 * i
                            at = HD * (h % 2)
                            ins = pe.matmul(bank[:, keys * i:keys * (i + 1)], qT[at:at + HD, h // 2, P * tile:P * (tile + 1)],
                                            kT[at:at + HD, h // 8, 0:keys], start=True, stop=True,
                                            tile_position=(at, 0))
                    if what == "pT":
                        pe.wait_ge(p_ready.sem, p_ready.at(l, job[1] + 1))
                        side_free(n)
                        ins = transposes(bank, [prob[:, job[1] % 2, P * i:P * (i + 1)] for i in range(4)])
                    if what == "av":
                        tile, h0, nh = GROUPS[job[1]]
                        m = AUXN["pT", job[1]]
                        pe.wait_ge(aux_taken[m % 2].sem, aux_taken[m % 2].at(l, m // 2 + 1))
                        side_free(n)
                        for i in range(nh):
                            at = HD * (h0 // 8)
                            for k in range(tile + 1):
                                ins = pe.matmul(bank[:, HD * i:HD * (i + 1)],
                                                probT[:, job[1] % 2, P * ((tile + 1) * i + k):P * ((tile + 1) * i + k + 1)],
                                                kv[:, k, P + at:P + at + HD], start=k == 0, stop=k == tile)
                    ins.then_inc(aux_done.sem, 1)

                for t in range(TOK):
                    pe.wait_ge(diag_ready.sem, diag_ready.at(l, t + 1))
                    side_free(t)
                    pe.matmul(side[t][:, 0:P], ones[:, :], diag[:, t, :], start=True, stop=True)\
                        .then_inc(aux_done.sem, 1)
                for g in range(NP):
                    if g == START["glu", 0]:
                        pe.wait_ge(yg_lo.sem, yg_lo.at(l, 4))
                    if g == START["out_a", 0]:
                        pe.wait_ge(gate_used.sem, gate_used.at(l, GATE_USE["glu", 1] + 1))
                    for name in "bc":
                        if g == START["out_" + name, 0]:
                            for i in (2, 3):
                                m = AUXN["yT", name, i]
                                pe.wait_ge(aux_taken[m % 2].sem, aux_taken[m % 2].at(l, m // 2 + 1))
                    piece(g)
                    k, off = divmod(g - S5_AT, 4)
                    if off == 0 and 0 <= k < TILES:
                        if k == 0:
                            pe.wait_ge(small_loaded.sem, small_loaded.at(l, 96))
                        s5_feed(k)
                    if off == 2 and 0 < k <= TILES:
                        if k == 1:
                            pe.wait_ge(c_scaled.sem, c_scaled.at(l, 1))
                        s5_out(k - 1)
                    for job in AUX_AFTER.get(g, ()):
                        side_job(job)
                for m in range(NXT):
                    n = AUXN["xT", m]
                    side_free(n)
                    x_transposes(l, m, n)


def constants():
    con = np.zeros((P, 128 + 256 + 32), np.float32)
    con[:, 0:128] = np.eye(P, dtype=np.float32)
    row, key = np.arange(P)[:, None], np.arange(2 * P)[None, :]
    ahead = row + P - key
    con[:, 128:384] = np.where((ahead >= 0) & (ahead < 128), 0.0, -1e30)
    inv = (500000.0 ** (-np.arange(0, 16, 2, dtype=np.float32) / np.float32(16))).astype(np.float32)
    ang = np.arange(SEQ, dtype=np.float32)[:, None] * inv[None, :]
    for i, f in enumerate((np.cos, np.sin)):
        tab = f(ang).astype(np.float32).reshape(TOK, P, 8).transpose(1, 0, 2)
        con[:, 384 + 16 * i:400 + 16 * i] = tab.reshape(P, 16)
    return con


def kernel(x, norm_w, w_in, ssm_a_re, ssm_a_im, ssm_log_dt, ssm_b_re, ssm_b_im, ssm_c_re, ssm_c_im, ssm_d,
           ssm_glu_w, ssm_glu_b, sg_ln_w, sg_ln_b, sg_w, sg_b, attn_sinks, w_branch_a, w_branch_b,
           w_branch_c, w_out, final_norm_w):
    import concourse.bacc as bacc
    from concourse.bass_utils import run_bass_kernel_spmd

    a = {k: np.asarray(v) for k, v in dict(
        x=x, norm_w=norm_w, w_in=w_in, a_re=ssm_a_re, a_im=ssm_a_im, log_dt=ssm_log_dt, b_re=ssm_b_re,
        b_im=ssm_b_im, c_re=ssm_c_re, c_im=ssm_c_im, d=ssm_d, glu=ssm_glu_w, glu_b=ssm_glu_b, ln_w=sg_ln_w,
        ln_b=sg_ln_b, sg_w=sg_w, sg_b=sg_b, sinks=attn_sinks, w_branch_a=w_branch_a, w_branch_b=w_branch_b,
        w_branch_c=w_branch_c, w_out=w_out, final=final_norm_w).items()}

    def columns(v):
        return v.reshape(DEPTH, -1, P).transpose(0, 2, 1)

    bT = np.zeros((DEPTH, 2, 4, 2, GROUP, WC, 2, STATE), np.float32)
    cT = np.zeros((DEPTH, 2, 2, STATE, WC, 4, 2, GROUP), np.float32)
    for part, (b, c) in enumerate((("b_re", "c_re"), ("b_im", "c_im"))):
        bb = a[b].reshape(DEPTH, WC, 4, 2, STATE, GROUP)
        cc = a[c].reshape(DEPTH, WC, 4, 2, GROUP, STATE)
        for two in range(2):
            bT[:, part, :, two, :, :, two, :] = bb[:, :, :, two].transpose(0, 2, 4, 1, 3)
            cT[:, part, two, :, :, :, two, :] = cc[:, :, :, two].transpose(0, 4, 1, 2, 3)
    bT = bT.reshape(DEPTH, 2, P, WC, P).transpose(0, 2, 1, 3, 4)
    cT = cT.reshape(DEPTH, 2, P, WC, P).transpose(0, 2, 1, 3, 4)

    def by_state(v):
        return v.reshape(DEPTH, TILES, P).transpose(0, 2, 1)

    log_dt = np.broadcast_to(a["log_dt"][:, :, None], (DEPTH, 2 * TILES, STATE))
    s5_par = np.concatenate([by_state(v) for v in (a["a_re"], a["a_im"], log_dt)], axis=2)
    cols = np.concatenate([
        columns(a["d"]), columns(a["glu_b"]), columns(np.roll(a["norm_w"], -1, axis=0)),
        a["sg_b"].transpose(0, 2, 1), np.broadcast_to(a["sinks"][:, None, :], (DEPTH, P, HEADS))], axis=2)
    ins = {
        "x": a["x"].reshape(SEQ, D), "w_in": a["w_in"], "glu": a["glu"], "w_branch_a": a["w_branch_a"],
        "w_branch_b": a["w_branch_b"], "w_branch_c": a["w_branch_c"], "w_out": a["w_out"],
        "first_norm": columns(a["norm_w"])[0], "bT": bT, "cT": cT, "s5_par": s5_par, "cols": cols,
        "ln_rows": np.concatenate([a["ln_w"], a["ln_b"]], axis=1)[:, None, :],
        "wsT": a["sg_w"].transpose(0, 3, 1, 2), "consts": constants(), "final_row": a["final"][None, :],
    }
    nc = bacc.Bacc("TRN2", target_bir_lowering=False, num_devices=1)
    arrays = {"in_" + k: np.ascontiguousarray(v) for k, v in ins.items()}
    ap = {k: nc.dram_tensor("in_" + k, arrays["in_" + k].shape, F32, kind="ExternalInput").ap() for k in ins}
    out = nc.dram_tensor("out", (SEQ, D), F32, kind="ExternalOutput").ap()
    w = {k: ap[k] for k in ("w_in", "glu", "w_branch_a", "w_branch_b", "w_branch_c", "w_out")}
    build(nc, ap["x"], w, ap["first_norm"], ap["bT"], ap["cT"], ap["s5_par"], ap["cols"], ap["ln_rows"],
          ap["wsT"], ap["consts"], ap["final_row"], out)
    got = run_bass_kernel_spmd(nc, [arrays], core_ids=[0])
    return got.results[0]["out"].reshape(1, SEQ, D)
```

```python
import math
from contextlib import ExitStack

import concourse.bass as bass
import numpy as np
from concourse import mybir

F32 = mybir.dt.float32
F32R = mybir.dt.float32r
I32 = mybir.dt.int32
ALU = mybir.AluOpType
ACT = mybir.ActivationFunctionType
AX_X = mybir.AxisListType.X

P = 128
DEPTH, SEQ, D = 2, 256, 2048
TOK = SEQ // P
KC = D // P
WID = D // 2
WC = WID // P
COLS = 512
HEADS, KV_HEADS, HD = 16, 2, 64
SG_HEADS = 8
STATE, GROUP = 64, 16
TILES = WID // GROUP * STATE // P
EPS = 1e-6
SCALE = HD ** -0.5

OFF = {}
_at = 0
for _name, _n in (("u_a", WID), ("z_a", WID), ("u_b", WID), ("v_b", WID), ("z_b", WID), ("q", WID),
                  ("kv", 2 * KV_HEADS * HD), ("z_c", WID), ("gates", 3 * D)):
    OFF[_name] = _at
    _at += _n
D_IN = _at


def plan():
    panels, pieces, start = [], [], {}

    def panel(kind, i, weight, chunks, col, cols=COLS):
        start[kind, i] = len(pieces)
        per = 2 * COLS // cols
        for c in range(0, chunks, per):
            pieces.append((weight, c, per, col, cols, kind, i, c + per == chunks))
        if kind != "kv":
            panels.append((kind, i))

    def pair(kind):
        for i in range(2):
            panel(kind, i, "w_in", KC, OFF[kind] + COLS * i)

    def branch(name, n):
        for j in range(D // COLS):
            panel("gate_" + name, j, "w_in", KC, OFF["gates"] + n * D + COLS * j)
            panel("out_" + name, j, "w_branch_" + name, WC, COLS * j)

    pair("u_a"), pair("v_b"), pair("u_b"), pair("z_b"), pair("q")
    panel("kv", 0, "w_in", KC, OFF["kv"], 2 * KV_HEADS * HD)
    branch("b", 1)
    pair("z_c")
    branch("c", 2)
    pair("z_a")
    panel("glu", 0, "glu", WC, 0), panel("glu", 1, "glu", WC, COLS)
    branch("a", 0)
    for j in range(D // COLS):
        panel("w_out", j, "w_out", KC, COLS * j)
    return panels, pieces, start


PANELS, PIECES, START = plan()
NP, NPAN = len(PIECES), len(PANELS)
PAN = {key: n for n, key in enumerate(PANELS)}
END = {}
for _g, _p in enumerate(PIECES):
    if _p[7]:
        END[_p[5], _p[6]] = _g
RAW, RING = 6, 3
assert NP % RAW == 0 and NP % RING == 0 and NPAN % 2 == 0

S5_AT = START["z_b", 0]
PAIRS = TILES // 2
GROUPS = []
for _h in (0, 8):
    GROUPS += [(0, _h + i, 4) for i in range(2)] + [(1, _h + 4 * (i // 2) + i % 2, 2) for i in range(4)]
ATT_AT, ATT_STEP = START["out_b", 0] + 4, 3
SCORES_AT, PT_AT, AV_AT = 0, 4, 7


RSTD_AT = 9


def aux_plan():
    jobs = {}

    def put(g, *job):
        jobs.setdefault(g, []).append(job)

    for m in range(2, KC // 2):
        put(m - 2, "xT", m)
    for t in range(TOK):
        put(RSTD_AT, "rstd", t)
    mix = END["u_b", 1] + 5
    for i in range(4):
        put(mix + i, "mix", i)
    for i in range(4):
        put(END["z_b", i // 2] + 6 + i % 2, "yT", "b", i)
    for i in range(4):
        put(END["kv", 0] + 8 + i // 2, "qT", i)
    put(END["kv", 0] + 10, "kT")
    last = ATT_AT + ATT_STEP * (len(GROUPS) - 1)
    for g in range(ATT_AT, last + AV_AT + 1):
        for what, at in (("pT", PT_AT), ("av", AV_AT), ("scores", SCORES_AT)):
            i, off = divmod(g - ATT_AT - at, ATT_STEP)
            if off == 0 and 0 <= i < len(GROUPS):
                put(g, what, i)
    for i in range(4):
        put(END["z_c", i // 2] + 5 + i % 2, "yT", "c", i)
    for i in range(6):
        put(END["gate_a", 3] + 1 + i // 2, "mT", i)
    for i in range(6, 8):
        put(END["out_a", 3] + 4, "mT", i)
    return jobs


AUX_AFTER = aux_plan()
AUX = [("xT", 0), ("xT", 1)]
for _g in sorted(AUX_AFTER):
    for _job in AUX_AFTER[_g]:
        if _job[0] == "qT" and _job[1] == 0:
            AUX.append(("kv",))
        AUX.append(_job)
AUXN = {job: n for n, job in enumerate(AUX)}
NAUX, NXT = len(AUX), KC // 2
assert NAUX % 2 == 0 and len(AUXN) == NAUX

DVE_STEPS, ACT_STEPS, POOL_STEPS, RAW_USES = 466, 62, 282, 16 * NP // RAW
GATE_USES = [k for k in PANELS if k[0] in ("z_b", "z_c", "glu") or k[0].startswith("gate")]
GATE_USE = {k: n for n, k in enumerate(GATE_USES)}


class Signal:

    def __init__(self, sem, per_layer=0, start=0):
        self.sem, self.per_layer, self.start = sem, per_layer, start

    def at(self, layer, n):
        return n if layer is None else layer * self.per_layer + (self.start + n)


class Steps:

    def __init__(self, event, layer=None):
        self.sem, self.event, self.layer, self.n = event.sem, event, layer, 0

    def one(self):
        self.n += 1
        return self.sem

    def so_far(self):
        return self.event.at(self.layer, self.n)


def build(nc, x, w, norm_cols, bT, cT, s5_par, cols, ln_rows, wsT, consts, final_row, out):
    ctx = ExitStack()
    xs = nc.dram_tensor("residual", [DEPTH, SEQ, D], F32, kind="Internal").ap()
    with ctx:
        def sb(name, shape, dt=F32):
            return ctx.enter_context(nc.sbuf_tensor(name, shape, dt))

        def sig(name, per_layer=0, start=0):
            return Signal(ctx.enter_context(nc.semaphore(name)), per_layer, start)

        raw = sb("raw", [P, RAW, 2 * COLS])
        w_hi = sb("w_hi", [P, RING, 2 * COLS], F32R)
        w_lo = sb("w_lo", [P, RING, 2 * COLS], F32R)
        h_hi = sb("h_hi", [P, KC, SEQ], F32R)
        h_lo = sb("h_lo", [P, KC, SEQ], F32R)
        y_hi = sb("y_hi", [P, WC, SEQ], F32R)
        y_lo = sb("y_lo", [P, WC, SEQ], F32R)
        wide = sb("wide", [P, TOK, D])
        v_b, u_b = (wide[:, :, :].rearrange("p t (b n) -> p b t n", b=2)[:, b] for b in range(2))
        gate = sb("gate", [P, TOK, COLS])
        att = sb("att", [P, 5632])
        q = att[:, 0:2048].rearrange("p (t n) -> p t n", t=TOK)
        kv = att[:, 2048:2560].rearrange("p (t n) -> p t n", t=TOK)
        kk = att[:, 2560:3072].rearrange("p (t g n) -> p t g n", t=TOK, g=KV_HEADS)
        qT = att[:, 3072:5120].rearrange("p (c n) -> p c n", c=8)
        kT = att[:, 5120:5632].rearrange("p (g n) -> p g n", g=KV_HEADS)
        ln_w, ln_b = att[:, 0:1024], att[:, 1024:2048]
        ws = att[:, 2048:3072].rearrange("p (h t) -> p h t", h=SG_HEADS)
        par = att[:, 3072:3072 + 96].rearrange("p (k j) -> p k j", k=3)
        scr = att[:, 3200:3200 + 640].rearrange("p (k j) -> p k j", k=20)
        z_a = att[:, 0:2048].rearrange("p (c n) -> p c n", c=WC)
        x_old = att[:, 0:4096].rearrange("p (t n) -> p t n", t=TOK)
        prob = sb("prob", [P, 2, 512])
        probT = sb("probT", [P, 2, 512])
        soft = sb("soft", [P, 5, 3, 4])
        u_a = sb("u_a", [P, WC, SEQ])
        fin = u_a[:, :, :].rearrange("p c n -> p (c n)")
        stack_raw = sb("stack_raw", [96, 2, 2, SEQ])
        stack = sb("stack", [96, 2, 2, SEQ], F32R)
        s5c = sb("s5c", [P, 2, WC, P])
        powers = sb("powers", [P, 2, 2, TILES, 16])
        step_par = sb("step_par", [P, 5, TILES])
        turn = sb("turn", [P, 2, 2, SEQ])
        pool_tmp = sb("pool_tmp", [P, 4, SEQ])
        prod = sb("prod", [P, 2, 2, SEQ])
        drive = sb("drive", [P, 2, SEQ])
        scan = sb("scan", [P, 2, SEQ])
        state = sb("state", [P, 2, 2, SEQ])
        con = sb("con", [P, 128 + 256 + 32])
        ident, mask = con[:, 0:128], con[:, 128:384]
        cos, sin = (con[:, 384 + 16 * i:400 + 16 * i].rearrange("p (t k) -> p t k", t=TOK) for i in range(2))
        ones = sb("ones", [P, P])
        col = sb("col", [P, 40])
        c_d, c_glu, c_sgb, c_sink = (col[:, a:b] for a, b in ((0, 8), (8, 16), (16, 24), (24, 40)))
        norm = sb("norm", [P, KC])
        ssq = sb("ssq", [P, TOK, 4])
        rstd = sb("rstd", [P, TOK])
        nwt = sb("nwt", [P, 6, TOK])
        nwt_i = sb("nwt_i", [P, 2, TOK], I32)
        two_k = sb("two_k", [P, TILES], I32)
        stats = sb("stats", [P, TOK, 2, 6])
        mv = sb("mv", [P, TOK, 2])
        ln_rs = sb("ln_rs", [P, TOK])
        diag = sb("diag", [P, TOK, P])
        rstd_bc = sb("rstd_bc", [P, SEQ])

        acc = [ctx.enter_context(nc.psum_tensor(f"acc{i}", [P, 512], F32)) for i in range(4)]
        bu = ctx.enter_context(nc.psum_tensor("bu", [P, 512], F32))
        ya = ctx.enter_context(nc.psum_tensor("ya", [P, 512], F32))
        side = [ctx.enter_context(nc.psum_tensor(f"side{i}", [P, 512], F32)) for i in range(2)]

        landed = [sig(f"landed{i}", RAW_USES) for i in range(RAW)]
        hi_ready = sig("hi_ready", NP)
        lo_ready = sig("lo_ready", NP)
        piece_done = sig("piece_done", NP, RING)
        taken = [sig(f"taken{i}", NPAN // 2, 1) for i in range(2)]
        aux_done = sig("aux_done", NAUX)
        aux_taken = [sig(f"aux_taken{i}", NAUX // 2, 1) for i in range(2)]
        x_ready = sig("x_ready", 4, 4)
        ssq_ready = sig("ssq_ready", 8)
        xt_hi = sig("xt_hi", 2 * NXT)
        diag_ready = sig("diag_ready", 2)
        part_hi = sig("part_hi", 16)
        gate_used = sig("gate_used", len(GATE_USES), 1)
        v_ready = sig("v_ready", TOK)
        rope_ready = sig("rope_ready", 1)
        max_ready = sig("max_ready", len(GROUPS))
        p_ready = sig("p_ready", len(GROUPS))
        za_ready = sig("za_ready", 2)
        yg_hi = sig("yg_hi", 4)
        yg_lo = sig("yg_lo", 4)
        ya_ready = sig("ya_ready", 2)
        ya_hi = sig("ya_hi", 2)
        s5_par_ready = sig("s5_par_ready", 1)
        c_scaled = sig("c_scaled", 1)
        turn_ready = sig("turn_ready", TILES)
        turn_used = sig("turn_used", TILES, 2)
        stack_loaded = sig("stack_loaded", 7 * 16 * PAIRS)
        stack_hi = sig("stack_hi", PAIRS)
        stack_lo = sig("stack_lo", 2 * PAIRS)
        bu_done = sig("bu_done", TILES)
        bu_read = sig("bu_read", TILES, 1)
        state_ready = sig("state_ready", TILES)
        state_used = sig("state_used", TILES, 2)
        y_read = sig("y_read", WC, 1)
        y_act = sig("y_act", WC)
        par_loaded = sig("par_loaded", 16)
        small_loaded = sig("small_loaded", 16 * 4)
        ws_masked = sig("ws_masked", 1)
        xold_loaded = sig("xold_loaded", 16)
        x_landed = [sig(f"x_landed{j}") for j in range(4)]
        norm_loaded = sig("norm_loaded", 16, 16)
        fin_loaded = sig("fin_loaded")
        x_stored = sig("x_stored", 64)
        con_loaded = sig("con_loaded")
        dve_set = sig("dve_set")
        alone = sig("alone")
        dve_step = sig("dve_step", DVE_STEPS)
        act_step = sig("act_step", ACT_STEPS)
        pool_step = sig("pool_step", POOL_STEPS)
        fin_ready = [sig(f"fin_ready{j}") for j in range(4)]
        fin_product = sig("fin_product")
        fin_product_1 = sig("fin_product_1")
        fin_rstd = sig("fin_rstd")
        stored = sig("stored")

        def accs(n):
            return acc[2 * (n % 2)], acc[2 * (n % 2) + 1]

        def is_channel_major(kind):
            return kind in ("u_a", "z_a", "glu")

        block = ctx.enter_context(nc.Block())

        @block.sync
        def _(sp):
            def load(g, layer):
                weight, c, n, at, width = PIECES[g][:5]
                src = w[weight][layer, P * c:P * (c + n), at:at + width]
                sp.dma_start(raw[:, g % RAW, 0:n * width].rearrange("p (c n) -> p c n", c=n),
                             src.rearrange("(c p) n -> p c n", p=P)).then_inc(landed[g % RAW].sem, 16)

            def load_stack(g, layer):
                p, off = divmod(g - S5_AT + 7, 8)
                if off or not 0 <= p < PAIRS:
                    return
                if p > 0:
                    sp.wait_ge(stack_lo.sem, stack_lo.at(layer, 2 * p))
                for i in range(2):
                    at, c = 32 * ((2 * p + i) % 4), (2 * p + i) // 4
                    for copy in range(3):
                        sp.dma_start(stack_raw[32 * copy:32 * copy + 32, 0, i, :], u_a[at:at + 32, c, :])\
                            .then_inc(stack_loaded.sem, 16)
                sp.dma_start(stack_raw[:, 1, :, :], bT[layer, :, 2 * p:2 * p + 2, :]).then_inc(stack_loaded.sem, 16)

            sp.dma_start(con[:, :], consts).then_inc(con_loaded.sem, 16)
            for g in range(RAW):
                if g < 5 and g != 1:
                    j = max(g - 1, 0)
                    at = slice(COLS * j, COLS * (j + 1))
                    sp.dma_start(wide[:, :, at], x[:, at].rearrange("(t p) n -> p t n", p=P))\
                        .then_inc(x_landed[j].sem, 16)
                load(g, 0)
            with sp.Fori(0, DEPTH - 1) as l:
                for g in range(NP):
                    sp.wait_ge(lo_ready.sem, lo_ready.at(l, g + 1))
                    sp.sem_inc(alone.sem, 1)
                    load((g + RAW) % NP, l if g + RAW < NP else l + 1)
                    load_stack(g, l)
            for g in range(NP - RAW):
                sp.wait_ge(lo_ready.sem, lo_ready.at(DEPTH - 1, g + 1))
                load(g + RAW, DEPTH - 1)
                load_stack(g, DEPTH - 1)
            sp.wait_ge(lo_ready.sem, DEPTH * NP)
            sp.dma_start(fin, final_row.broadcast_to([P, D])).then_inc(fin_loaded.sem, 16)
            for s in landed:
                sp.wait_ge(s.sem, DEPTH * RAW_USES)
            for j in (0, 2, 1, 3):
                at = slice(COLS * j, COLS * (j + 1))
                sp.wait_ge(fin_ready[j].sem, TOK)
                sp.dma_start(out[:, at].rearrange("(t p) n -> p t n", p=P), x_old[:, :, at]).then_inc(stored.sem, 16)
            sp.wait_ge(stored.sem, 64)

        @block.gpsimd
        def _(pool):
            pool.dma_start(norm[:, :], norm_cols[0]).then_inc(norm_loaded.sem, 16)
            for j in range(4):
                pool.wait_ge(x_landed[j].sem, 16)
                pool.sem_inc(x_ready.sem, 1)
            pool.wait_ge(dve_set.sem, 2)

            with pool.Fori(0, DEPTH) as l:
                st = Steps(pool_step, l)

                pool.wait_ge(x_ready.sem, x_ready.at(l, 0))
                pool.dma_start(par, s5_par[l].rearrange("p (k j) -> p k j", k=3)).then_inc(par_loaded.sem, 16)
                pool.dma_start(col[:, :], cols[l]).then_inc(small_loaded.sem, 16)
                for g, dst, src in ((2, s5c[:, :, :, :], cT[l]), (4, ws, wsT[l]),
                                    (7, att[:, 0:2048], ln_rows[l].broadcast_to([P, 2048]))):
                    pool.wait_ge(lo_ready.sem, lo_ready.at(l, g))
                    pool.sem_inc(alone.sem, 1)
                    pool.dma_start(dst, src).then_inc(small_loaded.sem, 16)
                for b in range(2):
                    pool.wait_ge(aux_taken[b].sem, aux_taken[b].at(l, NXT // 2))
                pool.sem_inc(alone.sem, 1)
                pool.dma_start(norm[:, :], norm_cols[1 - l]).then_inc(norm_loaded.sem, 16)
                pool.wait_ge(small_loaded.sem, small_loaded.at(l, 64))
                pool.sem_inc(alone.sem, 1)
                pool.affine_select(out=ws, in_=ws, compare_op=ALU.is_ge, fill=0.0, base=0,
                                   pattern=[[0, SG_HEADS], [1, P]], channel_multiplier=-1)\
                    .then_inc(ws_masked.sem, 1)

                for j in range(4):
                    pool.wait_ge(lo_ready.sem, lo_ready.at(l, 11 + 2 * j))
                    pool.wait_ge(x_ready.sem, x_ready.at(l, j + 1 - 4))
                    pool.sem_inc(alone.sem, 1)
                    pool.dma_start(xs[l, :, COLS * j:COLS * (j + 1)].rearrange("(t p) n -> p t n", p=P),
                                   wide[:, :, COLS * j:COLS * (j + 1)]).then_inc(x_stored.sem, 16)

                pool.wait_ge(s5_par_ready.sem, s5_par_ready.at(l, 1))
                pool.sem_inc(alone.sem, 1)
                tmp = pool_tmp[:, :, :].rearrange("p k n -> p (k n)")
                wc, wsn = tmp[:, 0:TILES], tmp[:, TILES:2 * TILES]
                pool.tensor_copy(wc, step_par[:, 1, :]).then_inc(st.one(), 1)
                pool.tensor_copy(wsn, step_par[:, 2, :]).then_inc(st.one(), 1)
                for part in (1, 0):
                    pool.wait_ge(st.sem, st.so_far())
                    pool.sem_inc(alone.sem, 1)
                    tab_c, tab_s = powers[:, part, 0], powers[:, part, 1]
                    pool.memset(tab_c[:, :, 0:1], 1.0).then_inc(st.one(), 1)
                    pool.memset(tab_s[:, :, 0:1], 0.0).then_inc(st.one(), 1)
                    for k in (1, 2, 4, 8):
                        bc = wc.rearrange("p (j o) -> p j o", o=1).broadcast_to([P, TILES, k])
                        bs = wsn.rearrange("p (j o) -> p j o", o=1).broadcast_to([P, TILES, k])
                        t1 = tmp[:, 256:256 + TILES * k].rearrange("p (j k) -> p j k", k=k)
                        t2 = tmp[:, 512:512 + TILES * k].rearrange("p (j k) -> p j k", k=k)
                        oc, os_ = tab_c[:, :, 0:k], tab_s[:, :, 0:k]
                        nc_, ns_ = tab_c[:, :, k:2 * k], tab_s[:, :, k:2 * k]
                        pool.wait_ge(st.sem, st.so_far())
                        pool.tensor_tensor(t1, oc, bc, ALU.mult).then_inc(st.one(), 1)
                        pool.tensor_tensor(t2, os_, bs, ALU.mult).then_inc(st.one(), 1)
                        pool.wait_ge(st.sem, st.so_far())
                        pool.tensor_tensor(nc_, t1, t2, ALU.subtract).then_inc(st.one(), 1)
                        pool.wait_ge(st.sem, st.so_far())
                        pool.tensor_tensor(t1, oc, bs, ALU.mult).then_inc(st.one(), 1)
                        pool.tensor_tensor(t2, os_, bc, ALU.mult).then_inc(st.one(), 1)
                        pool.wait_ge(st.sem, st.so_far())
                        pool.tensor_tensor(ns_, t1, t2, ALU.add).then_inc(st.one(), 1)
                        c2, s2, cs = (tmp[:, 768 + TILES * i:768 + TILES * (i + 1)] for i in range(3))
                        pool.tensor_tensor(c2, wc, wc, ALU.mult).then_inc(st.one(), 1)
                        pool.tensor_tensor(s2, wsn, wsn, ALU.mult).then_inc(st.one(), 1)
                        pool.tensor_tensor(cs, wc, wsn, ALU.mult).then_inc(st.one(), 1)
                        pool.wait_ge(st.sem, st.so_far())
                        pool.tensor_tensor(wc, c2, s2, ALU.subtract).then_inc(st.one(), 1)
                        pool.tensor_tensor(wsn, cs, cs, ALU.add).then_inc(st.one(), 1)
                pool.wait_ge(st.sem, st.so_far())

                def scale_c():
                    kr, ki = step_par[:, 3, :], step_par[:, 4, :]
                    for i in range(0, WC, 2):
                        js = slice(4 * i, 4 * i + 8)
                        kr_b = kr[:, js].rearrange("p (j o) -> p j o", o=1).broadcast_to([P, 8, 32])
                        ki_b = ki[:, js].rearrange("p (j o) -> p j o", o=1).broadcast_to([P, 8, 32])
                        cr = s5c[:, 0, i:i + 2, :].rearrange("p i (j c) -> p (i j) c", c=32)
                        ci = s5c[:, 1, i:i + 2, :].rearrange("p i (j c) -> p (i j) c", c=32)
                        t = [pool_tmp[:, k, :].rearrange("p (j c) -> p j c", c=32) for k in range(4)]
                        pool.tensor_tensor(t[0], cr, kr_b, ALU.mult).then_inc(st.one(), 1)
                        pool.tensor_tensor(t[1], ci, ki_b, ALU.mult).then_inc(st.one(), 1)
                        pool.tensor_tensor(t[2], ci, kr_b, ALU.mult).then_inc(st.one(), 1)
                        pool.tensor_tensor(t[3], cr, ki_b, ALU.mult).then_inc(st.one(), 1)
                        pool.wait_ge(st.sem, st.so_far())
                        pool.tensor_tensor(cr, t[0], t[1], ALU.subtract).then_inc(st.one(), 1)
                        pool.tensor_tensor(t[2], t[2], t[3], ALU.add).then_inc(st.one(), 1)
                        pool.wait_ge(st.sem, st.so_far())
                        pool.sem_inc(alone.sem, 1)
                        pool.tensor_scalar(ci, t[2], -1.0, 0.0, ALU.mult, ALU.add).then_inc(st.one(), 1)
                        pool.wait_ge(st.sem, st.so_far())
                    pool.sem_inc(c_scaled.sem, 1)

                def stack_low(p):
                    pool.wait_ge(stack_hi.sem, stack_hi.at(l, p + 1))
                    for kind in range(2):
                        at = slice(32 * kind, 32 * kind + 32)
                        pool.tensor_tensor(stack[at, kind], stack_raw[at, kind], stack[at, kind].bitcast(F32),
                                           ALU.subtract).then_inc(stack_lo.sem, 1)
                        pool.wait_ge(stack_lo.sem, stack_lo.at(l, 2 * p + kind + 1))

                for j in range(TILES):
                    if j > 0 and j % 2 == 0:
                        stack_low(j // 2)
                    ac, as_ = (powers[:, 0, k, j, :].rearrange("p (a o) -> p a o", o=1).broadcast_to([P, 16, 16])
                               for k in range(2))
                    bc, bs = (powers[:, 1, k, j, :].rearrange("p (o b) -> p o b", o=1).broadcast_to([P, 16, 16])
                              for k in range(2))
                    t = [pool_tmp[:, k, :].rearrange("p (a b) -> p a b", b=16) for k in range(4)]
                    pool.tensor_tensor(t[0], ac, bc, ALU.mult).then_inc(st.one(), 1)
                    pool.tensor_tensor(t[1], as_, bs, ALU.mult).then_inc(st.one(), 1)
                    pool.tensor_tensor(t[2], as_, bc, ALU.mult).then_inc(st.one(), 1)
                    pool.tensor_tensor(t[3], ac, bs, ALU.mult).then_inc(st.one(), 1)
                    pool.wait_ge(st.sem, st.so_far())
                    pool.wait_ge(turn_used.sem, turn_used.at(l, j - 1))
                    tc, ts = (turn[:, j % 2, k, :].rearrange("p (a b) -> p a b", b=16) for k in range(2))
                    pool.tensor_tensor(tc, t[0], t[1], ALU.subtract).then_inc(st.one(), 1)
                    pool.tensor_tensor(ts, t[2], t[3], ALU.add).then_inc(turn_ready.sem, 1)
                    pool.wait_ge(turn_ready.sem, turn_ready.at(l, j + 1))
                    if j == 1:
                        scale_c()
                        stack_low(0)
                pool.wait_ge(gate_used.sem, gate_used.at(l, GATE_USE["glu", 1] + 1))
                pool.wait_ge(x_stored.sem, x_stored.at(l, 64))
                pool.sem_inc(alone.sem, 1)
                pool.dma_start(x_old, xs[l].rearrange("(t p) n -> p t n", p=P)).then_inc(xold_loaded.sem, 16)
                assert st.n == POOL_STEPS, st.n
            pool.wait_ge(fin_loaded.sem, 16)
            at = slice(COLS, 2 * COLS)
            for t in range(TOK):
                pool.tensor_tensor(x_old[:, t, at], wide[:, t, at], fin[:, at], ALU.mult).then_inc(fin_product_1.sem, 1)
                pool.wait_ge(fin_product_1.sem, t + 1)
            pool.wait_ge(norm_loaded.sem, 16 * (DEPTH + 1))

        @block.scalar
        def _(act):
            def square_sums(l, j):
                act.wait_ge(x_ready.sem, x_ready.at(l, j + 1 - 4))
                for t in range(TOK):
                    act.activation(prob[:, t, :], wide[:, t, COLS * j:COLS * (j + 1)], ACT.Square,
                                   accum_out=ssq[:, t, j:j + 1]).then_inc(ssq_ready.sem, 1)
                    act.wait_ge(ssq_ready.sem, ssq_ready.at(l, 2 * j + t + 1))

            act.wait_ge(dve_set.sem, 2)
            with act.Fori(0, DEPTH) as l:
                st = Steps(act_step, l)

                def split(g):
                    _, _, n, _, width = PIECES[g][:5]
                    act.wait_ge(landed[g % RAW].sem, landed[g % RAW].at(l, 16 * (g // RAW + 1)))
                    act.wait_ge(piece_done.sem, piece_done.at(l, g + 1 - RING))
                    act.activation(w_hi[:, g % RING, :], raw[:, g % RAW, :], ACT.Copy).then_inc(hi_ready.sem, 1)

                def norm_hi(m):
                    n = AUXN["xT", m]
                    act.wait_ge(aux_done.sem, aux_done.at(l, n + 1))
                    for c in range(2):
                        act.activation(h_hi[:, 2 * m + c, :], side[n % 2][:, SEQ * c:SEQ * (c + 1)], ACT.Copy,
                                       scale=norm[:, 2 * m + c:2 * m + c + 1]).then_inc(xt_hi.sem, 1)

                def by_token(kind, i, func, dst):
                    n = PAN[kind, i]
                    act.wait_ge(piece_done.sem, piece_done.at(l, END[kind, i] + 1))
                    act.activation(dst[0], accs(n)[0][:, :], func, scale=rstd[:, 0:1]).then_inc(st.one(), 1)
                    act.activation(dst[1], accs(n)[1][:, :], func, scale=rstd[:, 1:2])\
                        .then_inc(taken[n % 2].sem, 1)

                def halves(t, i):
                    return [t[:, k, COLS * i:COLS * (i + 1)] for k in range(TOK)]

                def side_hi(job, dst):
                    n = AUXN[job]
                    act.wait_ge(aux_done.sem, aux_done.at(l, n + 1))
                    act.activation(dst, side[n % 2][:, :].rearrange("p (c n) -> p c n", c=2), ACT.Copy)\
                        .then_inc(part_hi.sem, 1)

                def side_copy(job, dst):
                    n = AUXN[job]
                    act.wait_ge(aux_done.sem, aux_done.at(l, n + 1))
                    act.activation(dst, side[n % 2][:, :], ACT.Copy).then_inc(aux_taken[n % 2].sem, 1)

                def exps(i):
                    tile, h0, nh = GROUPS[i]
                    b, keys = i % 2, P * (tile + 1)
                    act.wait_ge(max_ready.sem, max_ready.at(l, i + 1))
                    for k in range(nh):
                        pr = prob[:, b, keys * k:keys * (k + 1)]
                        act.activation(pr, pr, ACT.Exp, bias=soft[:, 1, i % 3, k:k + 1],
                                           accum_out=soft[:, 3, i % 3, k:k + 1]).then_inc(st.one(), 1)
                    act.activation(soft[:, 4, i % 3, 0:nh], soft[:, 2, i % 3, 0:nh], ACT.Exp).then_inc(p_ready.sem, 1)

                act.activation(prob[:, 0, 0:2], ones[:, 0:2], ACT.Copy).then_inc(st.one(), 1)
                act.wait_ge(st.sem, st.so_far())
                for g in range(NP):
                    split(g)
                    if g == 0:
                        act.wait_ge(norm_loaded.sem, norm_loaded.at(l, 0))
                    if g < NXT:
                        norm_hi(g)
                    if 1 <= g <= 4:
                        square_sums(l, g - 1)
                    if g == END["v_b", 0]:
                        act.wait_ge(diag_ready.sem, diag_ready.at(l, 2))
                        act.wait_ge(small_loaded.sem, small_loaded.at(l, 64))
                    for kind, func, dst in (("v_b", ACT.Gelu_apprx_tanh, v_b), ("u_b", ACT.Gelu_apprx_tanh, u_b),
                                            ("q", ACT.Copy, q)):
                        for i in range(2):
                            if g == END[kind, i] + RING:
                                if kind == "v_b" and i == 0:
                                    act.wait_ge(x_stored.sem, x_stored.at(l, 64))
                                if kind == "q":
                                    act.wait_ge(aux_taken[1].sem, aux_taken[1].at(l, (AUXN["mix", 3] + 1) // 2))
                                    act.wait_ge(aux_taken[0].sem, aux_taken[0].at(l, (AUXN["mix", 3] + 1) // 2))
                                by_token(kind, i, func, halves(dst, i))
                    for kind, i in GATE_USES:
                        if kind != "glu" and g == END[kind, i] + RING:
                            act.wait_ge(gate_used.sem, gate_used.at(l, GATE_USE[kind, i]))
                            by_token(kind, i, ACT.Silu if kind[0] == "z" else ACT.Sigmoid,
                                     [gate[:, k, :] for k in range(TOK)])
                    if g == END["kv", 0] + RING:
                        n = AUXN["kv",]
                        act.wait_ge(aux_done.sem, aux_done.at(l, n + 1))
                        act.activation(kv[:, 0, :], side[n % 2][:, 0:256], ACT.Copy, scale=rstd[:, 0:1]).then_inc(st.one(), 1)
                        act.activation(kv[:, 1, :], side[n % 2][:, 256:512], ACT.Copy, scale=rstd[:, 1:2])\
                            .then_inc(aux_taken[n % 2].sem, 1)
                    for job in AUX_AFTER.get(g - 2, ()):
                        if job[0] == "yT":
                            side_hi(job, y_hi[:, 2 * job[2]:2 * job[2] + 2, :])
                        if job[0] == "mT":
                            side_hi(job, h_hi[:, 2 * job[1]:2 * job[1] + 2, :])
                        if job[0] == "qT":
                            side_copy(job, qT[:, 2 * job[1]:2 * job[1] + 2, :].rearrange("p c n -> p (c n)"))
                        if job[0] == "kT":
                            side_copy(job, kT.rearrange("p g n -> p (g n)"))
                        if job[0] == "pT":
                            side_copy(job, probT[:, job[1] % 2, :])
                    i, off = divmod(g - ATT_AT - 3, ATT_STEP)
                    if off == 0 and 0 <= i < len(GROUPS):
                        exps(i)
                    p, off = divmod(g - S5_AT + 1, 8)
                    if off == 0 and 0 <= p < PAIRS:
                        act.wait_ge(stack_loaded.sem, stack_loaded.at(l, 112 * (p + 1)))
                        if p > 0:
                            act.wait_ge(bu_done.sem, bu_done.at(l, 2 * p))
                        act.activation(stack[:, :, :, :], stack_raw[:, :, :, :], ACT.Copy).then_inc(stack_hi.sem, 1)
                    i, off = divmod(g - S5_AT - 26, 16)
                    if off == 0 and 0 <= i < WC:
                        act.wait_ge(y_read.sem, y_read.at(l, i + 1))
                        act.activation(u_a[:, i, :], u_a[:, i, :], ACT.Gelu_apprx_tanh).then_inc(y_act.sem, 1)
                    for i in range(2):
                        if g == END["z_a", i] + RING + 1:
                            act.wait_ge(taken[PAN["z_a", i] % 2].sem, taken[PAN["z_a", i] % 2].at(l, PAN["z_a", i] // 2 + 1))
                            za = z_a[:, 4 * i:4 * i + 4, :]
                            act.activation(za, za, ACT.Silu).then_inc(za_ready.sem, 1)
                    for i in range(4):
                        if g == END["out_c", 3] + RING + 1 + i:
                            act.wait_ge(y_act.sem, y_act.at(l, WC))
                            act.activation(y_hi[:, 2 * i:2 * i + 2, :], u_a[:, 2 * i:2 * i + 2, :], ACT.Copy)\
                                .then_inc(yg_hi.sem, 1)

                    def glu_gate(i):
                        n = PAN["glu", i]
                        act.wait_ge(gate_used.sem, gate_used.at(l, GATE_USE["glu", i]))
                        act.wait_ge(piece_done.sem, piece_done.at(l, END["glu", i] + 1))
                        g4 = gate[:, :, :].rearrange("p t (c n) -> p (t c) n", n=SEQ)
                        for c in range(4):
                            ins = act.activation(g4[:, c, :], accs(n)[c // 2][:, SEQ * (c % 2):SEQ * (c % 2 + 1)],
                                                 ACT.Sigmoid, bias=c_glu[:, 4 * i + c:4 * i + c + 1])
                            if c < 3:
                                ins.then_inc(st.one(), 1)
                        ins.then_inc(taken[n % 2].sem, 1)

                    def ya_high(i):
                        act.wait_ge(ya_ready.sem, ya_ready.at(l, i + 1))
                        act.wait_ge(piece_done.sem, piece_done.at(l, END["glu", 1] + 1))
                        act.activation(y_hi[:, 4 * i:4 * i + 4, :],
                                       gate[:, :, :].rearrange("p t (c n) -> p (t c) n", n=SEQ), ACT.Copy)\
                            .then_inc(ya_hi.sem, 1)

                    if g == END["glu", 0] + RING:
                        glu_gate(0)
                    if g == END["glu", 1] + RING:
                        ya_high(0)
                        glu_gate(1)
                    if g == END["glu", 1] + RING + 2:
                        ya_high(1)
                assert st.n == ACT_STEPS, st.n
            for j in range(4):
                square_sums(DEPTH, j)
            act.wait_ge(fin_rstd.sem, 1)
            for j in range(2):
                act.wait_ge((fin_product, fin_product_1)[j].sem, TOK)
                at = slice(COLS * j, COLS * (j + 1))
                for t in range(TOK):
                    act.activation(x_old[:, t, at], x_old[:, t, at], ACT.Copy, scale=rstd[:, t:t + 1])\
                        .then_inc(fin_ready[j].sem, 1)

        @block.vector
        def _(dve):
            def new_x(l, st, j):
                n = PAN["w_out", j]
                dve.wait_ge(piece_done.sem, piece_done.at(l, END["w_out", j] + 1))
                for t in range(TOK):
                    at = slice(COLS * j, COLS * (j + 1))
                    ins = dve.tensor_tensor(wide[:, t, at], accs(n)[t][:, :], x_old[:, t, at], ALU.add)
                    if t == 0:
                        ins.then_inc(st.one(), 1)
                ins.then_inc(taken[n % 2].sem, 1)
                dve.wait_ge(taken[n % 2].sem, taken[n % 2].at(l, n // 2 + 1))
                dve.sem_inc(x_ready.sem, 1)

            def norm_lo(l, st, m):
                n = AUXN["xT", m]
                dve.wait_ge(xt_hi.sem, xt_hi.at(l, 2 * m + 2))
                for c in range(2):
                    ins = dve.scalar_tensor_tensor(
                        h_lo[:, 2 * m + c, :], side[n % 2][:, SEQ * c:SEQ * (c + 1)],
                        norm[:, 2 * m + c:2 * m + c + 1], h_hi[:, 2 * m + c, :].bitcast(F32),
                        ALU.mult, ALU.subtract)
                    if c == 0:
                        ins.then_inc(st.one(), 1)
                ins.then_inc(aux_taken[n % 2].sem, 1)

            def rsqrt(st, dst, src):
                dve.tensor_scalar(nwt[:, 1, :], src, -0.5, None, ALU.mult, ALU.bypass).then_inc(st.one(), 1)
                dve.tensor_scalar(nwt_i[:, 0, :], src.bitcast(I32), 1, None, ALU.logical_shift_right).then_inc(st.one(), 1)
                dve.wait_ge(st.sem, st.so_far())
                dve.tensor_scalar(nwt_i[:, 1, :], nwt_i[:, 0, :], -1.0, float(0x5F3759DF), ALU.mult, ALU.add).then_inc(st.one(), 1)
                dve.wait_ge(st.sem, st.so_far())
                y = nwt_i[:, 1, :].bitcast(F32)
                for k in range(3):
                    yield
                    dve.tensor_tensor(nwt[:, 2, :], y, y, ALU.mult).then_inc(st.one(), 1)
                    dve.wait_ge(st.sem, st.so_far())
                    dve.tensor_tensor(nwt[:, 3, :], nwt[:, 1, :], nwt[:, 2, :], ALU.mult).then_inc(st.one(), 1)
                    dve.wait_ge(st.sem, st.so_far())
                    to = dst if k == 2 else nwt[:, 4 + k % 2, :]
                    dve.scalar_tensor_tensor(to, nwt[:, 3, :], 1.5, y, ALU.add, ALU.mult).then_inc(st.one(), 1)
                    dve.wait_ge(st.sem, st.so_far())
                    y = to

            def row_rstd(l, st):
                dve.wait_ge(ssq_ready.sem, ssq_ready.at(DEPTH if l is None else l, 8))
                dve.tensor_reduce(nwt[:, 0, :], ssq[:, :, :], AX_X, ALU.add).then_inc(st.one(), 1)
                dve.wait_ge(st.sem, st.so_far())
                dve.tensor_scalar(nwt[:, 0, :], nwt[:, 0, :], 1.0 / D, EPS, ALU.mult, ALU.add).then_inc(st.one(), 1)
                dve.wait_ge(st.sem, st.so_far())
                yield from rsqrt(st, rstd[:, :], nwt[:, 0, :])

            dve.memset(ones[:, :], 1.0).then_inc(dve_set.sem, 1)
            dve.memset(nwt[:, :, :], 0.0).then_inc(dve_set.sem, 1)
            dve.sem_inc(gate_used.sem, 1)
            dve.sem_inc(turn_used.sem, 2)
            dve.sem_inc(bu_read.sem, 1)
            dve.sem_inc(y_read.sem, 1)
            dve.sem_inc(aux_taken[0].sem, 1)
            dve.sem_inc(aux_taken[1].sem, 1)

            dve.wait_ge(con_loaded.sem, 16)
            dve.wait_ge(dve_set.sem, 2)
            with dve.Fori(0, DEPTH) as l:
                st = Steps(dve_step, l)

                def split(g):
                    dve.wait_ge(hi_ready.sem, hi_ready.at(l, g + 1))
                    dve.tensor_tensor(w_lo[:, g % RING, :], raw[:, g % RAW, :], w_hi[:, g % RING, :].bitcast(F32),
                                      ALU.subtract).then_inc(lo_ready.sem, 1)

                def was_taken(kind, i):
                    dve.wait_ge(taken[PAN[kind, i] % 2].sem, taken[PAN[kind, i] % 2].at(l, PAN[kind, i] // 2 + 1))

                def by_channel(kind, i, dst):
                    n = PAN[kind, i]
                    dve.wait_ge(piece_done.sem, piece_done.at(l, END[kind, i] + 1))
                    for b in range(2):
                        ins = dve.tensor_tensor(
                            dst[:, 4 * i + 2 * b:4 * i + 2 * b + 2, :],
                            accs(n)[b][:, :].rearrange("p (c n) -> p c n", c=2),
                            rstd_bc[:, :].rearrange("p (o n) -> p o n", o=1).broadcast_to([P, 2, SEQ]), ALU.mult)
                        if b == 0:
                            ins.then_inc(st.one(), 1)
                    ins.then_inc(taken[n % 2].sem, 1)

                def opening():
                    yield from row_rstd(l, st)
                    yield
                    for t in range(TOK):
                        dve.tensor_scalar(diag[:, t, :], ident, rstd[:, t:t + 1], None, ALU.mult, ALU.bypass)\
                            .then_inc(diag_ready.sem, 1)

                def s5_parameters():
                    dve.wait_ge(par_loaded.sem, par_loaded.at(l, 16))
                    S = [scr[:, k, :] for k in range(20)]

                    def ts(o, a, s1, s2, op0, op1):
                        dve.tensor_scalar(o, a, s1, s2, op0, op1).then_inc(st.one(), 1), dve.wait_ge(st.sem, st.so_far())

                    def tt(o, a, b, op):
                        dve.tensor_tensor(o, a, b, op).then_inc(st.one(), 1), dve.wait_ge(st.sem, st.so_far())

                    def stt(o, a, s, b, op0, op1):
                        dve.scalar_tensor_tensor(o, a, s, b, op0, op1).then_inc(st.one(), 1), dve.wait_ge(st.sem, st.so_far())

                    magic = 12582912.0

                    def expm1(o, xin, scale_out):
                        xx, k, r, p = S[12:16]
                        yield
                        ts(xx, xin, -88.02, 88.0, ALU.max, ALU.min)
                        ts(k, xx, 1.0 / math.log(2.0), magic, ALU.mult, ALU.add)
                        ts(k, k, magic, None, ALU.subtract, ALU.bypass)
                        stt(r, k, -0.693359375, xx, ALU.mult, ALU.add)
                        stt(r, k, 2.12194440e-4, r, ALU.mult, ALU.add)
                        ts(p, r, 1.0 / math.factorial(8), None, ALU.mult, ALU.bypass)
                        yield
                        for n in range(7, 0, -1):
                            stt(p, p, 1.0 / math.factorial(n), r, ALU.add, ALU.mult)
                            if n == 4:
                                yield
                        ts(two_k[:, :], k, 127.0, 8388608.0, ALU.add, ALU.mult)
                        pw = two_k[:, :].bitcast(F32)
                        tt(p, p, pw, ALU.mult)
                        if scale_out:
                            tt(o, p, pw, ALU.add)
                        else:
                            stt(o, pw, -1.0, p, ALU.add, ALU.add)

                    re, im, log_dt = par[:, 0, :], par[:, 1, :], par[:, 2, :]
                    dt, m, th, k, r, z, z2, s, cm, t = S[0:10]
                    yield from expm1(dt, log_dt, True)
                    yield
                    tt(t, re, dt, ALU.mult)
                    yield from expm1(m, t, False)
                    yield
                    tt(th, im, dt, ALU.mult)
                    ts(k, th, 1.0 / (2 * math.pi), magic, ALU.mult, ALU.add)
                    ts(k, k, magic, None, ALU.subtract, ALU.bypass)
                    p1 = 6.28125
                    p2 = float(np.round((2 * math.pi - p1) * 2.0 ** 20) / 2.0 ** 20)
                    p3 = 2 * math.pi - p1 - p2
                    stt(r, k, -p1, th, ALU.mult, ALU.add)
                    stt(r, k, -p2, r, ALU.mult, ALU.add)
                    stt(r, k, -p3, r, ALU.mult, ALU.add)
                    yield
                    ts(z, r, 0.25, None, ALU.mult, ALU.bypass)
                    tt(z2, z, z, ALU.mult)
                    ts(s, z2, -1.0 / math.factorial(11), None, ALU.mult, ALU.bypass)
                    for n, sign in ((9, 1.0), (7, -1.0), (5, 1.0), (3, -1.0)):
                        stt(s, s, sign / math.factorial(n), z2, ALU.add, ALU.mult)
                        if n == 7:
                            yield
                    stt(s, s, 1.0, z, ALU.add, ALU.mult)
                    yield
                    ts(cm, z2, 1.0 / math.factorial(12), None, ALU.mult, ALU.bypass)
                    for n, sign in ((10, -1.0), (8, 1.0), (6, -1.0), (4, 1.0), (2, -1.0)):
                        stt(cm, cm, sign / math.factorial(n), z2, ALU.add, ALU.mult)
                        if n == 6:
                            yield
                    for _ in range(2):
                        yield
                        stt(t, cm, 1.0, s, ALU.add, ALU.mult)
                        tt(cm, s, s, ALU.mult)
                        ts(cm, cm, -2.0, None, ALU.mult, ALU.bypass)
                        ts(s, t, 2.0, None, ALU.mult, ALU.bypass)
                    ts(step_par[:, 0, :], m, 1.0, None, ALU.add, ALU.bypass)
                    ts(step_par[:, 1, :], cm, 1.0, None, ALU.add, ALU.bypass)
                    ts(step_par[:, 2, :], s, 1.0, None, ALU.mult, ALU.bypass)
                    yield
                    l_re, l_im, inv, a, b = S[10], S[11], S[16], S[17], S[18]
                    tt(t, m, cm, ALU.mult)
                    tt(l_re, m, cm, ALU.add)
                    tt(l_re, l_re, t, ALU.add)
                    stt(l_im, m, 1.0, s, ALU.add, ALU.mult)
                    yield
                    tt(a, re, re, ALU.mult)
                    tt(b, im, im, ALU.mult)
                    tt(a, a, b, ALU.add)
                    dve.reciprocal(inv, a).then_inc(st.one(), 1), dve.wait_ge(st.sem, st.so_far())
                    yield
                    tt(a, l_re, re, ALU.mult)
                    tt(b, l_im, im, ALU.mult)
                    tt(a, a, b, ALU.add)
                    tt(step_par[:, 3, :], a, inv, ALU.mult)
                    tt(a, l_im, re, ALU.mult)
                    tt(b, l_re, im, ALU.mult)
                    tt(a, a, b, ALU.subtract)
                    dve.tensor_tensor(step_par[:, 4, :], a, inv, ALU.mult).then_inc(s5_par_ready.sem, 1)

                def s5_tile(j, stage):
                    tc, ts = (turn[:, j % 2, k, :].rearrange("p (o n) -> p o n", o=1).broadcast_to([P, 2, SEQ])
                              for k in range(2))
                    if stage == 0:
                        dve.wait_ge(turn_ready.sem, turn_ready.at(l, j + 1))
                        dve.wait_ge(bu_done.sem, bu_done.at(l, j + 1))
                        if j > 0:
                            dve.wait_ge(state_ready.sem, state_ready.at(l, j))
                        drv = bu[:, :].rearrange("p (k n) -> p k n", k=2)
                        dve.tensor_tensor(prod[:, 0], drv, tc, ALU.mult).then_inc(st.one(), 1)
                        dve.tensor_tensor(prod[:, 1], drv, ts, ALU.mult).then_inc(bu_read.sem, 1)
                    if stage == 1:
                        dve.wait_ge(bu_read.sem, bu_read.at(l, j + 1))
                        dve.tensor_tensor(drive[:, 0], prod[:, 0, 0], prod[:, 1, 1], ALU.add).then_inc(st.one(), 1)
                        dve.tensor_tensor(drive[:, 1], prod[:, 0, 1], prod[:, 1, 0], ALU.subtract).then_inc(st.one(), 1)
                        dve.wait_ge(st.sem, st.so_far())
                        decay = step_par[:, 0, j:j + 1].broadcast_to([P, SEQ])
                        for k in range(2):
                            dve.tensor_tensor_scan(scan[:, k], decay, drive[:, k], 0.0, ALU.mult, ALU.add).then_inc(st.one(), 1)
                    if stage == 2:
                        dve.wait_ge(st.sem, st.so_far())
                        dve.tensor_tensor(prod[:, 0], scan[:, :, :], tc, ALU.mult).then_inc(st.one(), 1)
                        dve.tensor_tensor(prod[:, 1], scan[:, :, :], ts, ALU.mult).then_inc(turn_used.sem, 1)
                    if stage == 3:
                        dve.wait_ge(st.sem, st.so_far())
                        dve.wait_ge(turn_used.sem, turn_used.at(l, j + 1))
                        dve.wait_ge(state_used.sem, state_used.at(l, j - 1))
                        dve.tensor_tensor(state[:, j % 2, 0], prod[:, 0, 0], prod[:, 1, 1], ALU.subtract).then_inc(st.one(), 1)
                        dve.tensor_tensor(state[:, j % 2, 1], prod[:, 0, 1], prod[:, 1, 0], ALU.add)\
                            .then_inc(state_ready.sem, 1)

                def layer_norm():
                    for t in range(TOK):
                        for i in range(2):
                            dve.bn_stats(stats[:, t, i, :], v_b[:, t, COLS * i:COLS * (i + 1)]).then_inc(st.one(), 1)
                        yield
                    dve.wait_ge(st.sem, st.so_far())
                    dve.sem_inc(alone.sem, 1)
                    for t in range(TOK):
                        dve.bn_aggr(mv[:, t, :], stats[:, t, :, :]).then_inc(st.one(), 1)
                    dve.wait_ge(st.sem, st.so_far())
                    dve.tensor_scalar(ln_rs[:, :], mv[:, :, 1], EPS, None, ALU.add, ALU.bypass).then_inc(st.one(), 1)
                    dve.wait_ge(st.sem, st.so_far())
                    yield
                    yield from rsqrt(st, ln_rs[:, :], ln_rs[:, :])
                    for t in range(TOK):
                        yield
                        dve.scalar_tensor_tensor(v_b[:, t, :], v_b[:, t, :], mv[:, t, 0:1], ln_w,
                                                 ALU.subtract, ALU.mult).then_inc(st.one(), 1)
                    for t in range(TOK):
                        yield
                        dve.wait_ge(st.sem, st.so_far())
                        dve.scalar_tensor_tensor(v_b[:, t, :], v_b[:, t, :], ln_rs[:, t:t + 1], ln_b,
                                                 ALU.mult, ALU.add).then_inc(v_ready.sem, 1)

                def mixed(i):
                    n, t, h0 = AUXN["mix", i], i // 2, 4 * (i % 2)
                    dve.wait_ge(aux_done.sem, aux_done.at(l, n + 1))
                    for h in range(4):
                        at = slice(P * (h0 + h), P * (h0 + h + 1))
                        ins = dve.scalar_tensor_tensor(u_b[:, t, at], side[n % 2][:, P * h:P * (h + 1)],
                                                       c_sgb[:, h0 + h:h0 + h + 1], u_b[:, t, at],
                                                       ALU.add, ALU.mult)
                        if h < 3:
                            ins.then_inc(st.one(), 1)
                    ins.then_inc(aux_taken[n % 2].sem, 1)

                def times_gate(kind, i, dst):
                    was_taken(kind, i)
                    if kind == "z_b":
                        for n in (AUXN["mix", 2], AUXN["mix", 3]):
                            dve.wait_ge(aux_taken[n % 2].sem, aux_taken[n % 2].at(l, n // 2 + 1))
                    for t in range(TOK):
                        at = dst[:, t, COLS * i:COLS * (i + 1)]
                        ins = dve.tensor_tensor(at, at, gate[:, t, :], ALU.mult)
                        if t == 0:
                            ins.then_inc(st.one(), 1)
                    ins.then_inc(gate_used.sem, 1)

                def side_lo(job, dst, hi, nth):
                    n = AUXN[job]
                    dve.wait_ge(part_hi.sem, part_hi.at(l, nth + 1))
                    dve.tensor_tensor(dst, side[n % 2][:, :].rearrange("p (c n) -> p c n", c=2), hi.bitcast(F32),
                                      ALU.subtract).then_inc(aux_taken[n % 2].sem, 1)

                def rotary():
                    dve.wait_ge(aux_taken[AUXN["kv",] % 2].sem, aux_taken[AUXN["kv",] % 2].at(l, AUXN["kv",] // 2 + 1))
                    for src, nh in ((q.rearrange("p t (h d) -> p t h d", d=HD), HEADS),
                                    (kv[:, :, 0:P].rearrange("p t (h d) -> p t h d", d=HD), KV_HEADS)):
                        a, b = src[:, :, :, 0:8], src[:, :, :, 8:16]
                        c, s = (tab.rearrange("p t (o k) -> p t o k", o=1).broadcast_to([P, TOK, nh, 8])
                                for tab in (cos, sin))
                        t = [prob[:, k // 2, 256 * (k % 2):256 * (k % 2) + 16 * nh]
                             .rearrange("p (t h k) -> p t h k", t=TOK, k=8) for k in range(4)]
                        yield
                        dve.tensor_tensor(t[0], a, c, ALU.mult).then_inc(st.one(), 1)
                        dve.tensor_tensor(t[1], b, s, ALU.mult).then_inc(st.one(), 1)
                        dve.tensor_tensor(t[2], b, c, ALU.mult).then_inc(st.one(), 1)
                        dve.tensor_tensor(t[3], a, s, ALU.mult).then_inc(st.one(), 1)
                        dve.wait_ge(st.sem, st.so_far())
                        dve.tensor_tensor(a, t[0], t[1], ALU.subtract).then_inc(st.one(), 1)
                        dve.tensor_tensor(b, t[2], t[3], ALU.add).then_inc(st.one(), 1)
                        dve.wait_ge(st.sem, st.so_far())
                    yield
                    for t in range(TOK):
                        k_src = kv[:, t, 0:P].rearrange("p (g o d) -> p g o d", g=KV_HEADS, o=1)\
                            .broadcast_to([P, KV_HEADS, 2, HD])
                        dve.tensor_copy(kk[:, t, :, :].rearrange("p g (o d) -> p g o d", o=2), k_src).then_inc(st.one(), 1)
                    dve.wait_ge(st.sem, st.so_far())
                    dve.sem_inc(rope_ready.sem, 1)

                def softmax_max(i):
                    tile, h0, nh = GROUPS[i]
                    b, keys, n = i % 2, P * (tile + 1), AUXN["scores", i]
                    dve.wait_ge(aux_done.sem, aux_done.at(l, n + 1))
                    pr = prob[:, b, 0:nh * keys].rearrange("p (h k) -> p h k", h=nh)
                    m = mask[:, 256 - keys:256].rearrange("p (o k) -> p o k", o=1).broadcast_to([P, nh, keys])
                    dve.scalar_tensor_tensor(pr, side[n % 2][:, 0:nh * keys].rearrange("p (h k) -> p h k", h=nh),
                                             SCALE, m, ALU.mult, ALU.add).then_inc(aux_taken[n % 2].sem, 1)
                    dve.wait_ge(aux_taken[n % 2].sem, aux_taken[n % 2].at(l, n // 2 + 1))
                    sinks = c_sink[:, h0:h0 + 2 * nh - 1:2]
                    mx, neg, sk = soft[:, 0, i % 3, 0:nh], soft[:, 1, i % 3, 0:nh], soft[:, 2, i % 3, 0:nh]
                    dve.tensor_reduce(mx, pr, AX_X, ALU.max).then_inc(st.one(), 1)
                    dve.wait_ge(st.sem, st.so_far())
                    dve.tensor_tensor(mx, mx, sinks, ALU.max).then_inc(st.one(), 1)
                    dve.wait_ge(st.sem, st.so_far())
                    dve.tensor_tensor(sk, sinks, mx, ALU.subtract).then_inc(st.one(), 1)
                    dve.tensor_scalar(neg, mx, -1.0, None, ALU.mult, ALU.bypass).then_inc(max_ready.sem, 1)

                def attended(i):
                    tile, h0, nh = GROUPS[i]
                    b, n = i % 2, AUXN["av", i]
                    den = soft[:, 0, i % 3, 0:nh]
                    dve.wait_ge(p_ready.sem, p_ready.at(l, i + 1))
                    dve.tensor_tensor(den, soft[:, 3, i % 3, 0:nh], soft[:, 4, i % 3, 0:nh], ALU.add).then_inc(st.one(), 1)
                    dve.wait_ge(st.sem, st.so_far())
                    dve.reciprocal(soft[:, 2, i % 3, 0:nh], den).then_inc(st.one(), 1)
                    dve.wait_ge(st.sem, st.so_far())
                    dve.wait_ge(aux_done.sem, aux_done.at(l, n + 1))
                    dve.tensor_tensor(
                        q[:, tile, :].rearrange("p (h d) -> p h d", d=HD)[:, h0:h0 + 2 * nh - 1:2, :],
                        side[n % 2][:, 0:nh * HD].rearrange("p (h d) -> p h d", d=HD),
                        soft[:, 2, i % 3, 0:nh].rearrange("p (h o) -> p h o", o=1).broadcast_to([P, nh, HD]),
                        ALU.mult).then_inc(aux_taken[n % 2].sem, 1)

                def merge(name, j):
                    n = PAN["out_" + name, j]
                    dve.wait_ge(piece_done.sem, piece_done.at(l, END["out_" + name, j] + 1))
                    was_taken("gate_" + name, j)
                    for t in range(TOK):
                        at = wide[:, t, COLS * j:COLS * (j + 1)] if name == "b" else gate[:, t, :]
                        ins = dve.tensor_tensor(at, accs(n)[t][:, :], gate[:, t, :], ALU.mult)
                        if t == 0:
                            ins.then_inc(st.one(), 1)
                    ins.then_inc(taken[n % 2].sem, 1)
                    if name == "b":
                        dve.wait_ge(taken[n % 2].sem, taken[n % 2].at(l, n // 2 + 1))
                        dve.sem_inc(gate_used.sem, 1)

                def merge_add(name, j):
                    n = PAN["out_" + name, j]
                    dve.wait_ge(st.sem, st.so_far())
                    dve.wait_ge(taken[n % 2].sem, taken[n % 2].at(l, n // 2 + 1))
                    for t in range(TOK):
                        at = wide[:, t, COLS * j:COLS * (j + 1)]
                        ins = dve.tensor_tensor(at, at, gate[:, t, :], ALU.add)
                        if t == 0:
                            ins.then_inc(st.one(), 1)
                    ins.then_inc(gate_used.sem, 1)

                gate4 = gate[:, :, :].rearrange("p t (c n) -> p (t c) n", n=SEQ)

                def ya_products(i):
                    was_taken("glu", i)
                    dve.wait_ge(za_ready.sem, za_ready.at(l, i + 1))
                    dve.tensor_tensor(gate4, gate4, z_a[:, 4 * i:4 * i + 4, :], ALU.mult).then_inc(st.one(), 1)
                    dve.wait_ge(st.sem, st.so_far())
                    dve.tensor_tensor(gate4, gate4, u_a[:, 4 * i:4 * i + 4, :], ALU.mult).then_inc(ya_ready.sem, 1)

                def ya_low(i):
                    dve.wait_ge(ya_hi.sem, ya_hi.at(l, i + 1))
                    dve.tensor_tensor(y_lo[:, 4 * i:4 * i + 4, :], gate4,
                                      y_hi[:, 4 * i:4 * i + 4, :].bitcast(F32), ALU.subtract)\
                        .then_inc(gate_used.sem, 1)

                for g in range(NP):
                    split(g)
                    if g == 0:
                        dve.wait_ge(norm_loaded.sem, norm_loaded.at(l, 0))
                    if g < NXT:
                        norm_lo(l, st, g)
                    if g == RSTD_AT + 2:
                        for t in range(TOK):
                            n = AUXN["rstd", t]
                            dve.wait_ge(aux_done.sem, aux_done.at(l, n + 1))
                            dve.tensor_copy(rstd_bc[:, P * t:P * (t + 1)], side[n % 2][:, 0:P])\
                                .then_inc(aux_taken[n % 2].sem, 1)
                    if g == 5:
                        rstd_steps = opening()
                    if 5 <= g <= RSTD_AT + 1:
                        next(rstd_steps, None)
                    if g == 6:
                        steps = s5_parameters()
                    for i in range(2):
                        if g == END["u_a", i] + (RING if i else RING + 2):
                            if i == 0:
                                for t in range(TOK):
                                    n = AUXN["rstd", t]
                                    dve.wait_ge(aux_taken[n % 2].sem, aux_taken[n % 2].at(l, n // 2 + 1))
                            by_channel("u_a", i, u_a)
                        if g == END["z_b", i] + RING:
                            times_gate("z_b", i, u_b)
                        if g == END["z_c", i] + RING:
                            times_gate("z_c", i, q)
                        if g == END["z_a", i] + RING:
                            by_channel("z_a", i, z_a)
                    if g == END["v_b", 1] + RING + 1:
                        was_taken("v_b", 0), was_taken("v_b", 1)
                        dve.wait_ge(small_loaded.sem, small_loaded.at(l, 64))
                        assert not list(steps), "S5's parameters are not through"
                        steps = layer_norm()
                    if g == END["kv", 0] + RING:
                        assert not list(steps), "the LayerNorm is not through"
                        steps = rotary()
                    if g >= 6:
                        next(steps, None)
                    for job in AUX_AFTER.get(g - 2, ()):
                        if job[0] == "mix":
                            if job[1] == 0:
                                was_taken("u_b", 0), was_taken("u_b", 1)
                            mixed(job[1])
                        if job[0] == "yT":
                            m = job[2]
                            side_lo(job, y_lo[:, 2 * m:2 * m + 2, :], y_hi[:, 2 * m:2 * m + 2, :],
                                    m + (4 if job[1] == "c" else 0))
                        if job[0] == "mT":
                            m = job[1]
                            side_lo(job, h_lo[:, 2 * m:2 * m + 2, :], h_hi[:, 2 * m:2 * m + 2, :], 8 + m)
                        if job[0] == "scores":
                            softmax_max(job[1])
                        if job[0] == "av":
                            attended(job[1])
                    k, stage = divmod(g - S5_AT - 3, 4)
                    if 0 <= k < TILES:
                        s5_tile(k, stage)
                    i, off = divmod(g - S5_AT - 21, 16)
                    if off == 0 and 0 <= i < WC:
                        dve.wait_ge(state_used.sem, state_used.at(l, 4 * i + 4))
                        dve.scalar_tensor_tensor(u_a[:, i, :], u_a[:, i, :], c_d[:, i:i + 1], ya[:, 0:SEQ],
                                                 ALU.mult, ALU.add).then_inc(y_read.sem, 1)
                    for name in "bca":
                        for j in range(4):
                            if g == END["out_" + name, j] + RING:
                                merge(name, j)
                            if name != "b" and g == END["out_" + name, j] + RING + 1:
                                merge_add(name, j)
                    for i in range(4):
                        if g == END["out_c", 3] + RING + 1 + i:
                            dve.wait_ge(yg_hi.sem, yg_hi.at(l, i + 1))
                            dve.tensor_tensor(y_lo[:, 2 * i:2 * i + 2, :], u_a[:, 2 * i:2 * i + 2, :],
                                              y_hi[:, 2 * i:2 * i + 2, :].bitcast(F32), ALU.subtract)\
                                .then_inc(yg_lo.sem, 1)
                    if g == END["glu", 0] + RING:
                        ya_products(0)
                    if g == END["glu", 1] + RING:
                        ya_low(0)
                    if g == END["glu", 1] + RING + 1:
                        ya_products(1)
                    if g == END["glu", 1] + RING + 2:
                        ya_low(1)
                    if g == END["w_out", 0] + RING:
                        dve.wait_ge(xold_loaded.sem, xold_loaded.at(l, 16))
                    for j in range(3):
                        if g == END["w_out", j] + RING:
                            new_x(l, st, j)
                new_x(l, st, 3)
                assert st.n == DVE_STEPS, st.n

            last = Steps(sig("dve_last_step"))
            dve.wait_ge(fin_loaded.sem, 16)
            for t in range(TOK):
                dve.tensor_tensor(x_old[:, t, 0:COLS], wide[:, t, 0:COLS], fin[:, 0:COLS], ALU.mult)\
                    .then_inc(fin_product.sem, 1)
            for _ in row_rstd(None, last):
                pass
            dve.sem_inc(fin_rstd.sem, 1)
            for j in (2, 3):
                at = slice(COLS * j, COLS * (j + 1))
                for t in range(TOK):
                    dve.scalar_tensor_tensor(x_old[:, t, at], wide[:, t, at], rstd[:, t:t + 1], fin[:, at],
                                             ALU.mult, ALU.mult).then_inc(fin_ready[j].sem, 1)

        @block.tensor
        def _(pe):
            def transposes(dst, parts):
                for i, part in enumerate(parts):
                    ins = pe.transpose(dst[:, P * i:P * (i + 1)], part, ident)
                return ins

            pe.sem_inc(piece_done.sem, RING)
            pe.sem_inc(state_used.sem, 2)
            pe.sem_inc(taken[0].sem, 1)
            pe.sem_inc(taken[1].sem, 1)
            pe.wait_ge(con_loaded.sem, 16)
            pe.wait_ge(dve_set.sem, 2)

            with pe.Fori(0, DEPTH) as l:

                def side_free(n):
                    pe.wait_ge(aux_taken[n % 2].sem, aux_taken[n % 2].at(l, n // 2))

                def piece(g):
                    _, c0, nch, _, width, kind, i, last = PIECES[g]
                    slot, first = g % RING, c0 == 0
                    if kind == "kv":
                        banks = [side[AUXN["kv",] % 2]]
                    else:
                        n = PAN[kind, i]
                        banks = accs(n)
                    if first:
                        if kind == "kv":
                            side_free(AUXN["kv",])
                        else:
                            pe.wait_ge(taken[n % 2].sem, taken[n % 2].at(l, n // 2))
                    pe.wait_ge(lo_ready.sem, lo_ready.at(l, g + 1))
                    s_hi, s_lo = (y_hi, y_lo) if kind == "glu" or kind[:3] == "out" else (h_hi, h_lo)
                    for c in range(nch):
                        wh, wl = (t[:, slot, width * c:width * (c + 1)] for t in (w_hi, w_lo))
                        k = c0 + c
                        if kind == "w_out" and i == 0 and k % 2 == 0:
                            m = AUXN["mT", k // 2]
                            pe.wait_ge(aux_taken[m % 2].sem, aux_taken[m % 2].at(l, m // 2 + 1))
                        if kind == "u_a" and i == 0 and k % 2 == 0:
                            m = k // 2
                            pe.wait_ge(aux_taken[m % 2].sem, aux_taken[m % 2].at(l, m // 2 + 1))
                        if is_channel_major(kind):
                            for f in range(4):
                                o = banks[f // 2][:, SEQ * (f % 2):SEQ * (f % 2 + 1)]
                                at = slice(P * f, P * (f + 1))
                                for r, (a, b) in enumerate(((wh, s_hi), (wh, s_lo), (wl, s_hi))):
                                    ins = pe.matmul(o, a[:, at], b[:, k, :],
                                                    start=first and c == 0 and r == 0 and f % 2 == 0,
                                                    stop=last and c == nch - 1 and r == 2,
                                                    skip_group_check=True)
                        else:
                            for t in range(TOK):
                                o = banks[0][:, width * t:width * (t + 1)] if kind == "kv" else banks[t][:, :]
                                at = slice(P * t, P * (t + 1))
                                for r, (a, b) in enumerate(((s_hi, wh), (s_hi, wl), (s_lo, wh))):
                                    ins = pe.matmul(o, a[:, k, at], b,
                                                    start=first and c == 0 and r == 0 and
                                                    not (kind == "kv" and t == 1),
                                                    stop=last and c == nch - 1 and r == 2,
                                                    skip_group_check=kind == "kv")
                    ins.then_inc(piece_done.sem, 1)
                    if last and kind == "kv":
                        pe.wait_ge(piece_done.sem, piece_done.at(l, g + 1))
                        pe.sem_inc(aux_done.sem, 1)

                def s5_feed(k):
                    if k % 2 == 0:
                        pe.wait_ge(stack_lo.sem, stack_lo.at(l, k + 2))
                    pe.wait_ge(bu_read.sem, bu_read.at(l, k))
                    for part in range(2):
                        ins = pe.matmul(bu[:, SEQ * part:SEQ * (part + 1)], stack[:, 1, k % 2, P * part:P * (part + 1)],
                                        stack[:, 0, k % 2, :], start=True, stop=True)
                    ins.then_inc(bu_done.sem, 1)

                def s5_out(k):
                    at = 32 * (k % 4)
                    pe.wait_ge(state_ready.sem, state_ready.at(l, k + 1))
                    if k % 4 == 0:
                        pe.wait_ge(y_read.sem, y_read.at(l, k // 4))
                    for part in range(2):
                        ins = pe.matmul(ya[at:at + 32, 0:SEQ], s5c[:, part, k // 4, at:at + 32],
                                        state[:, k % 2, part, :], start=part == 0, stop=part == 1,
                                        tile_position=(0, at))
                    ins.then_inc(state_used.sem, 1)

                def side_job(job):
                    n = AUXN[job]
                    bank = side[n % 2]
                    what = job[0]
                    if what == "xT":
                        m = job[1]
                        pe.wait_ge(x_ready.sem, x_ready.at(l, m // 2 + 1 - 4))
                        side_free(n)
                        ins = transposes(bank, [wide[:, t, P * c:P * (c + 1)] for c in (2 * m, 2 * m + 1)
                                                for t in range(TOK)])
                    if what == "rstd":
                        pe.wait_ge(diag_ready.sem, diag_ready.at(l, job[1] + 1))
                        side_free(n)
                        ins = pe.matmul(bank[:, 0:P], ones[:, :], diag[:, job[1], :], start=True, stop=True)
                    if what == "mix":
                        t, h0 = job[1] // 2, 4 * (job[1] % 2)
                        pe.wait_ge(v_ready.sem, v_ready.at(l, TOK)), pe.wait_ge(ws_masked.sem, ws_masked.at(l, 1))
                        side_free(n)
                        for h in range(4):
                            ins = pe.matmul(bank[:, P * h:P * (h + 1)], ws[:, h0 + h, :],
                                            v_b[:, t, P * (h0 + h):P * (h0 + h + 1)], start=True, stop=True)
                    if what in ("yT", "mT"):
                        m = job[-1]
                        if what == "mT":
                            src = wide
                            pe.wait_ge(gate_used.sem, gate_used.at(l, GATE_USE["gate_a", m // 2] + 1))
                        else:
                            src = u_b if job[1] == "b" else q
                            pe.wait_ge(gate_used.sem, gate_used.at(l, GATE_USE["z_" + job[1], m // 2] + 1))
                        side_free(n)
                        ins = transposes(bank, [src[:, t, P * c:P * (c + 1)] for c in (2 * m, 2 * m + 1)
                                                for t in range(TOK)])
                    if what == "qT":
                        pe.wait_ge(rope_ready.sem, rope_ready.at(l, 1))
                        side_free(n)
                        ins = transposes(bank, [q[:, t, P * c:P * (c + 1)] for c in (2 * job[1], 2 * job[1] + 1)
                                                for t in range(TOK)])
                    if what == "kT":
                        side_free(n)
                        ins = transposes(bank, [kk[:, t, g, :] for g in range(KV_HEADS) for t in range(TOK)])
                    if what == "scores":
                        tile, h0, nh = GROUPS[job[1]]
                        keys = P * (tile + 1)
                        if job[1] == 0:
                            m = AUXN["kT",]
                            pe.wait_ge(aux_taken[m % 2].sem, aux_taken[m % 2].at(l, m // 2 + 1))
                            m = AUXN["qT", 3]
                            pe.wait_ge(aux_taken[m % 2].sem, aux_taken[m % 2].at(l, m // 2 + 1))
                        side_free(n)
                        for i in range(nh):
                            h = h0 + 2 * i
                            at = HD * (h % 2)
                            ins = pe.matmul(bank[:, keys * i:keys * (i + 1)], qT[at:at + HD, h // 2, P * tile:P * (tile + 1)],
                                            kT[at:at + HD, h // 8, 0:keys], start=True, stop=True,
                                            tile_position=(at, 0))
                    if what == "pT":
                        pe.wait_ge(p_ready.sem, p_ready.at(l, job[1] + 1))
                        side_free(n)
                        ins = transposes(bank, [prob[:, job[1] % 2, P * i:P * (i + 1)] for i in range(4)])
                    if what == "av":
                        tile, h0, nh = GROUPS[job[1]]
                        m = AUXN["pT", job[1]]
                        pe.wait_ge(aux_taken[m % 2].sem, aux_taken[m % 2].at(l, m // 2 + 1))
                        side_free(n)
                        for i in range(nh):
                            at = HD * (h0 // 8)
                            for k in range(tile + 1):
                                ins = pe.matmul(bank[:, HD * i:HD * (i + 1)],
                                                probT[:, job[1] % 2, P * ((tile + 1) * i + k):P * ((tile + 1) * i + k + 1)],
                                                kv[:, k, P + at:P + at + HD], start=k == 0, stop=k == tile)
                    ins.then_inc(aux_done.sem, 1)

                side_job(("xT", 0))
                side_job(("xT", 1))
                for g in range(NP):
                    if g == START["glu", 0]:
                        pe.wait_ge(yg_lo.sem, yg_lo.at(l, 4))
                    if g == START["out_a", 0]:
                        pe.wait_ge(gate_used.sem, gate_used.at(l, GATE_USE["glu", 1] + 1))
                    for name in "bc":
                        if g == START["out_" + name, 0]:
                            for i in (2, 3):
                                m = AUXN["yT", name, i]
                                pe.wait_ge(aux_taken[m % 2].sem, aux_taken[m % 2].at(l, m // 2 + 1))
                    piece(g)
                    k, off = divmod(g - S5_AT, 4)
                    if off == 0 and 0 <= k < TILES:
                        if k == 0:
                            pe.wait_ge(small_loaded.sem, small_loaded.at(l, 64))
                        s5_feed(k)
                    if off == 2 and 0 < k <= TILES:
                        if k == 1:
                            pe.wait_ge(c_scaled.sem, c_scaled.at(l, 1))
                        s5_out(k - 1)
                    for job in AUX_AFTER.get(g, ()):
                        side_job(job)


def constants():
    con = np.zeros((P, 128 + 256 + 32), np.float32)
    con[:, 0:128] = np.eye(P, dtype=np.float32)
    row, key = np.arange(P)[:, None], np.arange(2 * P)[None, :]
    ahead = row + P - key
    con[:, 128:384] = np.where((ahead >= 0) & (ahead < 128), 0.0, -1e30)
    inv = (500000.0 ** (-np.arange(0, 16, 2, dtype=np.float32) / np.float32(16))).astype(np.float32)
    ang = np.arange(SEQ, dtype=np.float32)[:, None] * inv[None, :]
    for i, f in enumerate((np.cos, np.sin)):
        tab = f(ang).astype(np.float32).reshape(TOK, P, 8).transpose(1, 0, 2)
        con[:, 384 + 16 * i:400 + 16 * i] = tab.reshape(P, 16)
    return con


def kernel(x, norm_w, w_in, ssm_a_re, ssm_a_im, ssm_log_dt, ssm_b_re, ssm_b_im, ssm_c_re, ssm_c_im, ssm_d,
           ssm_glu_w, ssm_glu_b, sg_ln_w, sg_ln_b, sg_w, sg_b, attn_sinks, w_branch_a, w_branch_b,
           w_branch_c, w_out, final_norm_w):
    import concourse.bacc as bacc
    from concourse.bass_utils import run_bass_kernel_spmd

    a = {k: np.asarray(v) for k, v in dict(
        x=x, norm_w=norm_w, w_in=w_in, a_re=ssm_a_re, a_im=ssm_a_im, log_dt=ssm_log_dt, b_re=ssm_b_re,
        b_im=ssm_b_im, c_re=ssm_c_re, c_im=ssm_c_im, d=ssm_d, glu=ssm_glu_w, glu_b=ssm_glu_b, ln_w=sg_ln_w,
        ln_b=sg_ln_b, sg_w=sg_w, sg_b=sg_b, sinks=attn_sinks, w_branch_a=w_branch_a, w_branch_b=w_branch_b,
        w_branch_c=w_branch_c, w_out=w_out, final=final_norm_w).items()}

    def columns(v):
        return v.reshape(DEPTH, -1, P).transpose(0, 2, 1)

    bT = np.zeros((DEPTH, 2, 4, 2, GROUP, WC, 2, STATE), np.float32)
    cT = np.zeros((DEPTH, 2, 2, STATE, WC, 4, 2, GROUP), np.float32)
    for part, (b, c) in enumerate((("b_re", "c_re"), ("b_im", "c_im"))):
        bb = a[b].reshape(DEPTH, WC, 4, 2, STATE, GROUP)
        cc = a[c].reshape(DEPTH, WC, 4, 2, GROUP, STATE)
        for two in range(2):
            bT[:, part, :, two, :, :, two, :] = bb[:, :, :, two].transpose(0, 2, 4, 1, 3)
            cT[:, part, two, :, :, :, two, :] = cc[:, :, :, two].transpose(0, 4, 1, 2, 3)
    bT = bT.reshape(DEPTH, 2, 4, 32, WC, P).transpose(0, 3, 4, 2, 1, 5).reshape(DEPTH, 32, TILES, 2 * P)
    bT = np.concatenate([bT, bT, bT], axis=1)
    cT = cT.reshape(DEPTH, 2, P, WC, P).transpose(0, 2, 1, 3, 4)

    def by_state(v):
        return v.reshape(DEPTH, TILES, P).transpose(0, 2, 1)

    log_dt = np.broadcast_to(a["log_dt"][:, :, None], (DEPTH, 2 * TILES, STATE))
    s5_par = np.concatenate([by_state(v) for v in (a["a_re"], a["a_im"], log_dt)], axis=2)
    cols = np.concatenate([
        columns(a["d"]), columns(a["glu_b"]), a["sg_b"].transpose(0, 2, 1), np.broadcast_to(a["sinks"][:, None, :], (DEPTH, P, HEADS))], axis=2)
    ins = {
        "x": a["x"].reshape(SEQ, D), "w_in": a["w_in"], "glu": a["glu"], "w_branch_a": a["w_branch_a"],
        "w_branch_b": a["w_branch_b"], "w_branch_c": a["w_branch_c"], "w_out": a["w_out"],
        "norm_cols": columns(a["norm_w"]), "bT": bT, "cT": cT, "s5_par": s5_par, "cols": cols,
        "ln_rows": np.concatenate([a["ln_w"], a["ln_b"]], axis=1)[:, None, :],
        "wsT": a["sg_w"].transpose(0, 3, 1, 2), "consts": constants(), "final_row": a["final"][None, :],
    }
    nc = bacc.Bacc("TRN2", target_bir_lowering=False, num_devices=1)
    arrays = {"in_" + k: np.ascontiguousarray(v) for k, v in ins.items()}
    ap = {k: nc.dram_tensor("in_" + k, arrays["in_" + k].shape, F32, kind="ExternalInput").ap() for k in ins}
    out = nc.dram_tensor("out", (SEQ, D), F32, kind="ExternalOutput").ap()
    w = {k: ap[k] for k in ("w_in", "glu", "w_branch_a", "w_branch_b", "w_branch_c", "w_out")}
    build(nc, ap["x"], w, ap["norm_cols"], ap["bT"], ap["cT"], ap["s5_par"], ap["cols"], ap["ln_rows"],
          ap["wsT"], ap["consts"], ap["final_row"], out)
    got = run_bass_kernel_spmd(nc, [arrays], core_ids=[0])
    return got.results[0]["out"].reshape(1, SEQ, D)
```
